# Optimizing a Trainium2 kernel written in Bass

```python
import math
import jax
import jax.numpy as jnp
from jax import lax
import numpy as np

D_MODEL = 1024
BATCH = 1
SEQ = 256
DEPTH = 2

MIX_WIDTH = D_MODEL
HEAD_DIM = 64
DA_WIDTH = MIX_WIDTH // 2
DA_HEADS = DA_WIDTH // (2 * HEAD_DIM)
SB_WIDTH = MIX_WIDTH - DA_WIDTH
SB_HEADS = SB_WIDTH // HEAD_DIM
ROPE_DIM = HEAD_DIM // 4
ROPE_THETA = 500000.0
Q_BLOCK = 128
N_GROUPS = 4
EXPERTS_PER_GROUP = 8
N_EXPERTS = N_GROUPS * EXPERTS_PER_GROUP
TOP_K_IN_GROUP = 2
EXPERT_FF = D_MODEL // 4
RMS_EPS = 1e-6
PROJ_WIDTH = 3 * DA_WIDTH + 3 * SB_WIDTH
SPLITS = [DA_WIDTH, 2 * DA_WIDTH, 3 * DA_WIDTH, 3 * DA_WIDTH + SB_WIDTH, 3 * DA_WIDTH + 2 * SB_WIDTH]

kernel_name = 'hybrid_diffattn_stickbreak_hmoe'

def rms_norm(x, g):
    xf = x.astype(jnp.float32)
    y = xf * lax.rsqrt(jnp.mean(xf * xf, axis=-1, keepdims=True) + RMS_EPS)
    return (y * g.astype(jnp.float32)).astype(x.dtype)

def split_heads(t, n_heads, head_dim):
    b, s, _ = t.shape
    return t.reshape(b, s, n_heads, head_dim).transpose(0, 2, 1, 3)

def merge_heads(t):
    b, h, s, d = t.shape
    return t.transpose(0, 2, 1, 3).reshape(b, s, h * d)

def rope_tables(seq):
    inv_freq = 1.0 / (ROPE_THETA ** (jnp.arange(0, ROPE_DIM, 2, dtype=jnp.float32) / ROPE_DIM))
    ang = jnp.arange(seq, dtype=jnp.float32)[:, None] * inv_freq[None, :]
    return jnp.cos(ang), jnp.sin(ang)

def partial_rope(t, cos, sin):
    half = ROPE_DIM // 2
    x1 = t[..., :half]
    x2 = t[..., half:ROPE_DIM]
    c = cos.astype(t.dtype)
    s = sin.astype(t.dtype)
    return jnp.concatenate([x1 * c - x2 * s, x2 * c + x1 * s, t[..., ROPE_DIM:]], axis=-1)

def to_query_blocks(q):
    b, h, s, d = q.shape
    return q.reshape(b, h, s // Q_BLOCK, Q_BLOCK, d).transpose(2, 0, 1, 3, 4)

def from_query_blocks(o):
    nb, b, h, qb, d = o.shape
    return o.transpose(1, 2, 0, 3, 4).reshape(b, h, nb * qb, d)

def diff_attention(q, k, v, lam):
    b, h2, s, d = q.shape
    h = h2 // 2
    scale = d ** -0.5
    kpos = jnp.arange(s)

    def block(args):
        qi, i = args
        sc = jnp.einsum('bhqd,bhkd->bhqk', qi, k).astype(jnp.float32) * scale
        qpos = i * Q_BLOCK + jnp.arange(Q_BLOCK)
        sc = jnp.where(kpos[None, :] <= qpos[:, None], sc, -jnp.inf)
        p = jax.nn.softmax(sc, axis=-1).reshape(b, h, 2, Q_BLOCK, s)
        a = p[:, :, 0] - lam * p[:, :, 1]
        return jnp.einsum('bhqk,bhkd->bhqd', a.astype(v.dtype), v)

    o = lax.map(block, (to_query_blocks(q), jnp.arange(s // Q_BLOCK)))
    return from_query_blocks(o)

def stick_breaking_attention(q, k, v):
    b, h, s, d = q.shape
    scale = d ** -0.5
    kpos = jnp.arange(s)

    def block(args):
        qi, i = args
        z = jnp.einsum('bhqd,bhkd->bhqk', qi, k).astype(jnp.float32) * scale
        qpos = i * Q_BLOCK + jnp.arange(Q_BLOCK)
        strict = kpos[None, :] < qpos[:, None]
        log_fail = jnp.where(strict, jax.nn.log_sigmoid(-z), 0.0)
        after = lax.cumsum(log_fail, axis=3, reverse=True) - log_fail
        log_a = jax.nn.log_sigmoid(z) + after
        a = jnp.where(strict, jnp.exp(log_a), 0.0)
        return jnp.einsum('bhqk,bhkd->bhqd', a.astype(v.dtype), v)

    o = lax.map(block, (to_query_blocks(q), jnp.arange(s // Q_BLOCK)))
    return from_query_blocks(o)

def hierarchical_moe(h, w_rg, b_rg, w_re, b_re, w_gate, w_up, w_down):
    def per_sequence(hs):
        n = hs.shape[0]
        g_prob = jax.nn.softmax((hs @ w_rg + b_rg).astype(jnp.float32), axis=-1)
        g_p, g_idx = lax.top_k(g_prob, 1)
        e_logits = (hs @ w_re + b_re).astype(jnp.float32).reshape(n, N_GROUPS, EXPERTS_PER_GROUP)
        idx = jnp.broadcast_to(g_idx[:, :, None], (n, 1, EXPERTS_PER_GROUP))
        e_in = jnp.take_along_axis(e_logits, idx, axis=1)[:, 0]
        e_top, e_idx = lax.top_k(e_in, TOP_K_IN_GROUP)
        w = g_p * jax.nn.softmax(e_top, axis=-1)
        expert_id = g_idx * EXPERTS_PER_GROUP + e_idx
        combine = jnp.sum(jax.nn.one_hot(expert_id, N_EXPERTS, dtype=jnp.float32) * w[..., None], axis=1)
        hg = jnp.einsum('sd,edf->sef', hs, w_gate)
        hu = jnp.einsum('sd,edf->sef', hs, w_up)
        act = jax.nn.silu(hg) * hu * combine.astype(hs.dtype)[..., None]
        return jnp.einsum('sef,efd->sd', act, w_down)

    return lax.map(per_sequence, h)

def setup_inputs(seed: int = 0) -> dict:
    key = jax.random.key(seed)
    ks = jax.random.split(key, 20)
    L, D = DEPTH, D_MODEL
    f32 = jnp.float32

    def normal(k, shape, scale):
        return jax.random.normal(k, shape, f32) * scale

    def gain(k, shape):
        return 1.0 + 0.02 * jax.random.normal(k, shape, f32)

    return {
        'x': normal(ks[0], (BATCH, SEQ, D), 1.0),
        'norm1_g': gain(ks[1], (L, D)),
        'w_in': normal(ks[2], (L, D, PROJ_WIDTH), D ** -0.5),
        'q_norm_g': gain(ks[3], (L, HEAD_DIM)),
        'k_norm_g': gain(ks[4], (L, HEAD_DIM)),
        'lambda_q1': normal(ks[5], (L, HEAD_DIM), 0.1),
        'lambda_k1': normal(ks[6], (L, HEAD_DIM), 0.1),
        'lambda_q2': normal(ks[7], (L, HEAD_DIM), 0.1),
        'lambda_k2': normal(ks[8], (L, HEAD_DIM), 0.1),
        'da_out_g': gain(ks[9], (L, 2 * HEAD_DIM)),
        'sb_out_g': gain(ks[10], (L, HEAD_DIM)),
        'w_out': normal(ks[11], (L, MIX_WIDTH, D), MIX_WIDTH ** -0.5),
        'norm2_g': gain(ks[12], (L, D)),
        'w_router_group': normal(ks[13], (L, D, N_GROUPS), D ** -0.5),
        'b_router_group': normal(ks[14], (L, N_GROUPS), 0.01),
        'w_router_expert': normal(ks[15], (L, D, N_EXPERTS), D ** -0.5),
        'b_router_expert': normal(ks[16], (L, N_EXPERTS), 0.01),
        'w_gate': normal(ks[17], (L, N_EXPERTS, D, EXPERT_FF), D ** -0.5),
        'w_up': normal(ks[18], (L, N_EXPERTS, D, EXPERT_FF), D ** -0.5),
        'w_down': normal(ks[19], (L, N_EXPERTS, EXPERT_FF, D), EXPERT_FF ** -0.5),
    }

def reference(x, norm1_g, w_in, q_norm_g, k_norm_g, lambda_q1, lambda_k1, lambda_q2, lambda_k2,
              da_out_g, sb_out_g, w_out, norm2_g, w_router_group, b_router_group,
              w_router_expert, b_router_expert, w_gate, w_up, w_down):
    _, s, _ = x.shape
    cos, sin = rope_tables(s)
    for l in range(DEPTH):
        lambda_init = 0.8 - 0.6 * math.exp(-0.3 * l)
        h = rms_norm(x, norm1_g[l])
        proj = h @ w_in[l]
        da_q, da_k, da_v, sb_q, sb_k, sb_v = jnp.split(proj, SPLITS, axis=-1)

        q = partial_rope(rms_norm(split_heads(da_q, 2 * DA_HEADS, HEAD_DIM), q_norm_g[l]), cos, sin)
        k = partial_rope(rms_norm(split_heads(da_k, 2 * DA_HEADS, HEAD_DIM), k_norm_g[l]), cos, sin)
        v = split_heads(da_v, DA_HEADS, 2 * HEAD_DIM)
        lam = (jnp.exp(jnp.sum(lambda_q1[l].astype(jnp.float32) * lambda_k1[l].astype(jnp.float32)))
               - jnp.exp(jnp.sum(lambda_q2[l].astype(jnp.float32) * lambda_k2[l].astype(jnp.float32)))
               + lambda_init)
        o_da = diff_attention(q, k, v, lam)
        o_da = merge_heads(rms_norm(o_da, da_out_g[l]) * (1.0 - lambda_init))

        o_sb = stick_breaking_attention(split_heads(sb_q, SB_HEADS, HEAD_DIM),
                                        split_heads(sb_k, SB_HEADS, HEAD_DIM),
                                        split_heads(sb_v, SB_HEADS, HEAD_DIM))
        o_sb = merge_heads(rms_norm(o_sb, sb_out_g[l]))

        x = x + jnp.concatenate([o_da, o_sb], axis=-1) @ w_out[l]

        h2 = rms_norm(x, norm2_g[l])
        x = x + hierarchical_moe(h2, w_router_group[l], b_router_group[l], w_router_expert[l],
                                 b_router_expert[l], w_gate[l], w_up[l], w_down[l])
    return x


_drawn_inputs = setup_inputs


def setup_inputs(seed=0):
    import zlib

    import numpy as np

    out = dict(_drawn_inputs(seed))
    spreads = {}
    factors = {'da_out_g': 2.68,
     'b_router_group': 7.639,
     'b_router_expert': 9.212,
     'sb_out_g': 3.746,
     'norm2_g': 3.092}
    for name, (base, spread) in spreads.items():
        noise = np.random.default_rng([zlib.crc32(name.encode()), seed]).standard_normal(out[name].shape)
        drawn = base * np.exp(spread * noise) if base else spread * noise
        out[name] = jnp.asarray(drawn.astype(out[name].dtype))
    for name, factor in factors.items():
        out[name] = (out[name] * factor).astype(out[name].dtype)
    return out
```

```python
import math
from contextlib import ExitStack

import concourse.bass as bass
import numpy as np
from concourse import mybir

F32 = mybir.dt.float32
I32 = mybir.dt.int32
ALU = mybir.AluOpType
ACT = mybir.ActivationFunctionType
AX = mybir.AxisListType

P = 128
D = 1024
SEQ = 256
DEPTH = 2
TT = SEQ // P
KC = D // P
HD = 64
PAIRS = 4
HALF = D // 2
GROUPS, PER_GROUP, EXPERTS = 4, 8, 32
FF = D // 4
FC = FF // P
LANES = 4
SLOTS = P // LANES
ROUNDS = SEQ // SLOTS
SETS = EXPERTS // LANES
ROPE = HD // 8
ROPE_THETA = 500000.0
EPS = 1e-6
SCALE = HD ** -0.5
NEG = -1e30
BIG = 64.0

DA_Q, DA_K, DA_V, SB_Q, SB_K, SB_V = range(6)
ORDER = [DA_Q, DA_K, SB_Q, SB_K, DA_V, SB_V]
XUNITS = len(ORDER) + 2

SB_ORDER = [4, 5, 0, 1, 2, 3]
DAS_BANK = [(0, 1), (2, 3), (0, 1)]
DAT_BANK = [6, 7, 6]
SB_BANK = [4, 5, 0, 1, 2, 3]
DAO_BANK = [7, 6]
SBO_BANK = [2, 3]
OT_BANK = [(2, 3), (6, 7)]
OP_BANK = [(4, 5), (0, 1)]
SC_BANK = [(6, 7), (0, 1)]

C_ID, C_GE, C_LT, C_ONE, C_MQ, C_MS, C_IOTA, C_REV, C_COS, C_SIN, C_END = np.cumsum(
    [0, P, P, P, P, 2 * P, 2 * P, P, EXPERTS, TT * ROPE, TT * ROPE]).tolist()


def shape_constants():
    c = np.zeros((P, C_END), np.float32)
    i = np.arange(P)
    c[:, C_ID:C_GE] = np.eye(P)
    c[:, C_GE:C_LT] = i[:, None] >= i[None, :]
    c[:, C_LT:C_ONE] = i[:, None] < i[None, :]
    c[:, C_ONE:C_MQ] = 1.0
    c[:, C_MQ + P:C_MS] = np.where(i[None, :] <= i[:, None], 0.0, NEG)
    c[:, C_MS:C_MS + P] = np.where(i[:, None] < i[None, :], 0.0, NEG)
    c[:, C_IOTA:C_REV] = i % SLOTS
    c[:, C_REV:C_COS] = BIG - np.arange(EXPERTS)
    freq = (1.0 / (np.float32(ROPE_THETA) ** (np.arange(0, 2 * ROPE, 2, dtype=np.float32) / (2 * ROPE))))
    angle = np.arange(SEQ, dtype=np.float32)[:, None] * freq.astype(np.float32)[None, :]
    angle = angle.reshape(TT, P, ROPE).transpose(1, 0, 2).reshape(P, TT * ROPE).astype(np.float64)
    c[:, C_COS:C_SIN] = np.cos(angle)
    c[:, C_SIN:C_END] = np.sin(angle)
    return c


def decoder(nc, const, x, norm1_g, w_in, q_norm_g, k_norm_g, lambda_q1, lambda_k1, lambda_q2, lambda_k2,
            da_out_g, sb_out_g, w_out, norm2_g, w_router_group, b_router_group, w_router_expert,
            b_router_expert, w_gate, w_up, w_down, out):
    with ExitStack() as ctx:
        def sb(name, shape, dt=F32):
            return ctx.enter_context(nc.sbuf_tensor(name, shape, dt))

        def sem(name):
            return ctx.enter_context(nc.semaphore(name))

        xbuf = sb("xbuf", [P, 2, KC, HALF])
        gubuf = sb("gubuf", [P, LANES, KC, 2, FF])
        dnbuf = sb("dnbuf", [P, LANES, FC * D])
        x_sb = sb("x_sb", [P, TT, D])
        xn = sb("xn", [P, TT, D])
        work = sb("work", [P, 8 * HALF])
        qkT = sb("qkT", [P, 4 * PAIRS * SEQ])
        v_sb = sb("v_sb", [P, TT, 2, HALF])
        cst = sb("cst", [P, C_END])
        g1 = sb("g1", [P, D])
        g2 = sb("g2", [P, D])
        wr = sb("wr", [P, KC, GROUPS + EXPERTS])
        br = sb("br", [P, GROUPS + EXPERTS])
        qkg = sb("qkg", [P, 2, HD])
        dag = sb("dag", [P, 2 * HD])
        sbg = sb("sbg", [P, HD])
        lamv = sb("lamv", [P, 4, HD])
        lams = sb("lams", [P, 4])
        ssq = sb("ssq", [P, TT])
        rstd = sb("rstd", [P, TT])
        hss = sb("hss", [P, 2 * 16])
        hr = sb("hr", [P, 2 * 16])
        rope = sb("rope", [P, 4, TT * 8 * ROPE])
        dmax = sb("dmax", [P, 3, 8])
        dsum = sb("dsum", [P, 3, 8])
        oss = sb("oss", [P, 2, 12])
        lg = sb("lg", [P, TT, GROUPS + EXPERTS])
        rs = sb("rs", [P, 8, TT])
        r4 = sb("r4", [P, 4, TT, GROUPS])
        em = sb("em", [P, TT, EXPERTS])
        ev = sb("ev", [P, TT, EXPERTS])
        oh1 = sb("oh1", [P, TT, EXPERTS])
        oh2 = sb("oh2", [P, TT, EXPERTS])
        asg = sb("asg", [P, TT, EXPERTS])
        wgt = sb("wgt", [P, TT, EXPERTS])
        pos = sb("pos", [P, TT, EXPERTS])
        posg = sb("posg", [P, TT, LANES])
        wgg = sb("wgg", [P, TT, LANES])
        cntf = sb("cntf", [P, SETS])
        cnt = sb("cnt", [P, SETS], I32)

        ident = cst[:, C_ID:C_GE]
        tri_ge = cst[:, C_GE:C_LT]
        tri_lt = cst[:, C_LT:C_ONE]
        ones = cst[:, C_ONE:C_MQ]

        def over(ap, n):
            return ap.unsqueeze(1).broadcast_to([P, n, ap.shape[1]])

        hT = work[:, 0:KC * SEQ].rearrange("p (k t) -> p k t", k=KC)
        stage = work[:, KC * SEQ:].rearrange("p (b t c) -> p b t c", b=2, t=TT)
        sp = work[:, 0:6 * HALF].rearrange("p (u c) -> p u c", u=6)
        scratch = dnbuf[:, :, :].rearrange("p a b -> p (a b)")
        s_da = scratch[:, 0:6 * HALF].rearrange("p (u e c) -> p u e c", u=3, e=2)
        zm = scratch[:, 6 * HALF:12 * HALF].rearrange("p (u c) -> p u c", u=6)
        aT = scratch[:, 12 * HALF:15 * HALF].rearrange("p (u b c) -> p u b c", u=3, b=4)
        sq = scratch[:, 6 * HALF:8 * HALF]
        osq = scratch[:, 0:4 * HALF].rearrange("p (u c) -> p u c", u=4)
        qk = qkT[:, :].rearrange("p (i a t) -> p i a t", i=4, a=PAIRS)
        at = [0]

        def take(n):
            at[0] += n
            return qkT[:, at[0] - n:at[0]]
        hgT = take(KC * P).rearrange("p (k s) -> p k s", k=KC)
        y = take(D)
        eg, rg, tg = take(FF), take(FF), take(FF)
        act_sb = take(FF)
        actT = take(FF).rearrange("p (c s) -> p c s", c=FC)
        sel = take(TT * P).rearrange("p (t s) -> p t s", t=TT)
        selw = take(TT * P).rearrange("p (t s) -> p t s", t=TT)
        selwT = take(TT * P).rearrange("p (t s) -> p t s", t=TT)

        ps = [ctx.enter_context(nc.psum_tensor(f"bank{i}", [P, HALF], F32)) for i in range(8)]

        const_in, x_in, par_in = sem("const_in"), sem("x_in"), sem("par_in")
        xslot_in = [sem(f"xslot_in{i}") for i in range(2)]
        gu_in = [sem(f"gu_in{j}") for j in range(LANES)]
        dn_in = [sem(f"dn_in{j}") for j in range(LANES)]
        out_done = sem("out_done")
        norm_r, h_ready = sem("norm_r"), sem("h_ready")
        hT_ps, hT_d, hT_a = sem("hT_ps"), sem("hT_d"), sem("hT_a")
        proj_ps, proj_out, xslot_used = sem("proj_ps"), sem("proj_out"), sem("xslot_used")
        qk_ss, qk_r, qk_normed = sem("qk_ss"), sem("qk_r"), sem("qk_normed")
        qkT_ps, qkT_d, qkT_a = sem("qkT_ps"), sem("qkT_d"), sem("qkT_a")
        lam_dot, lam_exp = sem("lam_dot"), sem("lam_exp")
        da_ps, da_max, da_exp, da_mix = sem("da_ps"), sem("da_max"), sem("da_exp"), sem("da_mix")
        daT_ps, daT_out, da_o = sem("daT_ps"), sem("daT_out"), sem("da_o")
        sb_ps, sb_abs, sb_ln, sb_sp = sem("sb_ps"), sem("sb_abs"), sem("sb_ln"), sem("sb_sp")
        sb_cum, sb_arg, sb_a, sb_o = sem("sb_cum"), sem("sb_arg"), sem("sb_a"), sem("sb_o")
        o_sq, o_ss, o_r, o_ready = sem("o_sq"), sem("o_ss"), sem("o_r"), sem("o_ready")
        oT_ps, oT_d, oT_a = sem("oT_ps"), sem("oT_d"), sem("oT_a")
        oproj_ps, x_attn = sem("oproj_ps"), sem("x_attn")
        lg_ps, rt_diff, rt_exp, rt_asg = sem("lg_ps"), sem("rt_diff"), sem("rt_exp"), sem("rt_asg")
        pos_ps, routed = sem("pos_ps"), sem("routed")
        sel_ready, gathered, selwT_ps = sem("sel_ready"), sem("gathered"), sem("selwT_ps")
        hg_d, hg_a, selwT_out = sem("hg_d"), sem("hg_a"), sem("selwT_out")
        gu_ps, gate_exp, act_out = sem("gu_ps"), sem("gate_exp"), sem("act_out")
        actT_ps, actT_out, dn_ps = sem("actT_ps"), sem("actT_out"), sem("dn_ps")
        y_d, y_a, sc_ps, x_moe = sem("y_d"), sem("y_a"), sem("sc_ps"), sem("x_moe")
        gu_used, dn_used = sem("gu_used"), sem("dn_used")
        PE_ROUND = (gathered, selwT_ps, gu_ps, actT_ps, dn_ps, sc_ps)
        DVE_ROUND = (sel_ready, hg_d, selwT_out, act_out, actT_out, y_d, x_moe)

        def bcast(v, n):
            return v.unsqueeze(0).broadcast_to([P, n])

        def params(l):
            yield g1[:, :], bcast(norm1_g[l], D)
            yield qkg[:, 0, :], bcast(q_norm_g[l], HD)
            yield qkg[:, 1, :], bcast(k_norm_g[l], HD)
            for n, v in enumerate((lambda_q1, lambda_k1, lambda_q2, lambda_k2)):
                yield lamv[:, n, :], bcast(v[l], HD)
            yield dag[:, :], bcast(da_out_g[l], 2 * HD)
            yield sbg[:, :], bcast(sb_out_g[l], HD)
            yield g2[:, :], bcast(norm2_g[l], D)
            yield wr[:, :, 0:GROUPS], w_router_group[l].rearrange("(p k) n -> p k n", k=KC)
            yield wr[:, :, GROUPS:], w_router_expert[l].rearrange("(p k) n -> p k n", k=KC)
            yield br[:, 0:GROUPS], bcast(b_router_group[l], GROUPS)
            yield br[:, GROUPS:], bcast(b_router_expert[l], EXPERTS)
        N_PAR = 14 * 16

        w_gate_e = w_gate.rearrange("l e (p k) f -> (l e) p k f", k=KC)
        w_up_e = w_up.rearrange("l e (p k) f -> (l e) p k f", k=KC)
        w_down_e = w_down.rearrange("l e (p c) d -> (l e) p (c d)", c=FC)

        R_ALL = SETS * ROUNDS

        block = ctx.enter_context(nc.Block())

        @block.sync
        def _(sp_):
            sp_.dma_start(x_sb[:, :, :], x[0].rearrange("(t p) d -> p t d", p=P)).then_inc(x_in, 16)

            def load_x(l, i):
                n = l * XUNITS + i
                if n >= 2:
                    sp_.wait_ge(xslot_used, n - 1)
                if i < len(ORDER):
                    c = ORDER[i] * HALF
                    src = w_in[l, :, c:c + HALF]
                else:
                    c = (i - len(ORDER)) * HALF
                    src = w_out[l, :, c:c + HALF]
                sp_.dma_start(xbuf[:, i % 2], src.rearrange("(k p) c -> p k c", p=P)).then_inc(xslot_in[i % 2], 16)

            def load_gu(e, j):
                sp_.dma_start(gubuf[:, j, :, 0, :], w_gate_e[e + j]).then_inc(gu_in[j], 16)
                sp_.dma_start(gubuf[:, j, :, 1, :], w_up_e[e + j]).then_inc(gu_in[j], 16)

            def load_dn(e, j):
                sp_.dma_start(dnbuf[:, j, :], w_down_e[e + j]).then_inc(dn_in[j], 16)

            load_x(0, 0)
            load_x(0, 1)
            for l in range(DEPTH):
                load_x(l, 2)
                load_x(l, 3)
                if l:
                    sp_.wait_ge(gu_used, l * SETS)
                for j in range(LANES):
                    load_gu(l * EXPERTS, j)
                for i in range(4, XUNITS):
                    load_x(l, i)
                sp_.wait_ge(x_attn, (l + 1) * 2 * TT)
                for j in range(LANES):
                    load_dn(l * EXPERTS, j)
                if l + 1 < DEPTH:
                    load_x(l + 1, 0)
                    load_x(l + 1, 1)
                with sp_.Fori(1, SETS) as g:
                    e = sp_.snap(g * LANES + l * EXPERTS)
                    sp_.wait_ge(gu_used, g + l * SETS)
                    for j in range(LANES):
                        load_gu(e, j)
                    sp_.wait_ge(dn_used, g + l * SETS)
                    for j in range(LANES):
                        load_dn(e, j)
            sp_.wait_ge(x_moe, DEPTH * R_ALL)
            sp_.dma_start(out[0].rearrange("(t p) d -> p t d", p=P), x_sb[:, :, :]).then_inc(out_done, 16)
            sp_.wait_ge(out_done, 16)

        @block.gpsimd
        def _(pool):
            nc.gpsimd.dma_start(cst[:, :], const).then_inc(const_in, 16)
            for l in range(DEPTH):
                if l:
                    pool.wait_ge(routed, l)
                for dst, src in params(l):
                    nc.gpsimd.dma_start(dst, src).then_inc(par_in, 16)

        @block.scalar
        def _(act):
            act.preload_act_table_set("natural_log_exp_and_others")

            def scales(out_ap, in_ap, width):
                nc.scalar.activation(out_ap, in_ap, ACT.Ln, bias=EPS, scale=1.0 / width)
                act.drain()
                return nc.scalar.activation(out_ap, out_ap, ACT.Exp, scale=-0.5)

            def norm(l):
                for t in range(TT):
                    nc.scalar.activation(xn[:, t, :], x_sb[:, t, :], ACT.Square, accum_out=ssq[:, t:t + 1])
                act.drain()
                scales(rstd[:, :], ssq[:, :], D).then_inc(norm_r, 1)

            def hT_half(n):
                for t in range(TT):
                    act.wait_ge(hT_ps, n * 2 * TT + 2 * t + 2)
                    nc.scalar.copy(hT[:, 4:8, t * P:(t + 1) * P],
                                   ps[2 * t + 1][:, :].rearrange("p (k c) -> p k c", k=4)).then_inc(hT_a, 1)

            def proj(l, i):
                for t in range(TT):
                    n = l * 12 + 2 * i + t
                    act.wait_ge(proj_ps, n + 1)
                    if i in (2, 3):
                        act.wait_ge(qkT_ps, l * 8 + 2 * (i - 2) + 2)
                    dst = stage[:, i % 2, t, :] if i < 4 else v_sb[:, t, i - 4, :]
                    nc.scalar.copy(dst, ps[4 + (2 * i + t) % 4][:, :]).then_inc(proj_out, 1)

            def qk_scale(l, i):
                act.wait_ge(qk_ss, l * 2 + i + 1)
                scales(hr[:, i * 16:i * 16 + 16], hss[:, i * 16:i * 16 + 16], HD).then_inc(qk_r, 1)

            def qkT_half(l, i):
                act.wait_ge(qkT_ps, l * 8 + 2 * i + 2)
                nc.scalar.copy(qk[:, i, :, P:2 * P], ps[2 * (i % 2) + 1][:, :].rearrange("p (a c) -> p a c", a=PAIRS))\
                  .then_inc(qkT_a, 1)

            def softmax_exp(l, u):
                act.wait_ge(da_max, l * 3 + u + 1)
                keys = P if u == 0 else 2 * P
                heads = HALF // keys
                for e in range(2):
                    for h in range(heads):
                        c = e * heads + h
                        s = s_da[:, u, e, h * keys:(h + 1) * keys]
                        last = nc.scalar.activation(s, s, ACT.Exp, bias=dmax[:, u, c:c + 1],
                                                    accum_out=dsum[:, u, c:c + 1])
                act.drain().then_inc(da_exp, 1)

            def softplus_ln(l, ws):
                for w in ws:
                    n = SB_ORDER.index(w)
                    act.wait_ge(sb_abs, l * 6 + n + 1)
                    nc.scalar.activation(sp[:, w, :], sp[:, w, :], ACT.Exp)
                act.drain()
                for w in ws:
                    nc.scalar.activation(sp[:, w, :], sp[:, w, :], ACT.Ln, bias=1.0).then_inc(sb_ln, 1)

            def daT_copy(l, u):
                act.wait_ge(daT_ps, l * 3 + u + 1)
                nc.scalar.copy(aT[:, u], ps[DAT_BANK[u]][:, :].rearrange("p (b c) -> p b c", b=4)).then_inc(daT_out, 1)

            def break_exp(l, w):
                act.wait_ge(sb_arg, l * 6 + SB_ORDER.index(w) + 1)
                nc.scalar.activation(zm[:, w, :], zm[:, w, :], ACT.Exp).then_inc(sb_a, 1)

            def expert_round(first, n):
                act.wait_ge(gathered, n + 1)
                nc.scalar.copy(hgT[:, 4:8, :], ps[1][:, :].rearrange("p (k s) -> p k s", k=4)).then_inc(hg_a, 1)
                act.wait_ge(gu_ps, n + 1)
                nc.scalar.activation(eg, ps[2][:, 0:FF], ACT.Exp, scale=-1.0).then_inc(gate_exp, 1)
                act.wait_ge(dn_ps, n + 1)
                nc.scalar.copy(y[:, HALF:], ps[5][:, :]).then_inc(y_a, 1)

            for l in range(DEPTH):
                if l == 0:
                    act.wait_ge(x_in, 16)
                else:
                    act.wait_ge(x_moe, l * R_ALL)
                norm(l)
                hT_half(2 * l)
                act.wait_ge(lam_dot, l + 1)
                nc.scalar.activation(lams[:, 2:4], lams[:, 0:2], ACT.Exp).then_inc(lam_exp, 1)
                proj(l, 0)
                qk_scale(l, 0)
                proj(l, 1)
                qk_scale(l, 1)
                qkT_half(l, 0)
                proj(l, 2)
                qkT_half(l, 1)
                proj(l, 3)
                qkT_half(l, 2)
                qkT_half(l, 3)
                softmax_exp(l, 0)
                softmax_exp(l, 1)
                proj(l, 4)
                softmax_exp(l, 2)
                proj(l, 5)
                softplus_ln(l, (4, 5))
                daT_copy(l, 0)
                daT_copy(l, 1)
                softplus_ln(l, (0, 1))
                softplus_ln(l, (2, 3))
                break_exp(l, 4)
                break_exp(l, 5)
                daT_copy(l, 2)
                for w in range(4):
                    break_exp(l, w)
                act.wait_ge(da_o, (l + 1))
                for t in range(TT):
                    nc.scalar.activation(osq[:, t, :], ps[DAO_BANK[t]][:, :], ACT.Square)
                act.wait_ge(sb_o, (l + 1))
                for t in range(TT):
                    nc.scalar.activation(osq[:, 2 + t, :], ps[SBO_BANK[t]][:, :], ACT.Square)
                act.drain().then_inc(o_sq, 1)
                act.wait_ge(o_ss, l + 1)
                scales(oss[:, 1, 0:8], oss[:, 0, 0:8], 2 * HD)
                scales(hr[:, 0:16], hss[:, 0:16], HD)
                act.drain().then_inc(o_r, 1)
                for t in range(TT):
                    act.wait_ge(oT_ps, l * 4 + 2 * t + 2)
                    nc.scalar.copy(hT[:, 4:8, t * P:(t + 1) * P],
                                   ps[OT_BANK[t][1]][:, :].rearrange("p (k c) -> p k c", k=4)).then_inc(oT_a, 1)
                act.wait_ge(x_attn, (l + 1) * 2 * TT)
                norm(l)
                hT_half(2 * l + 1)
                act.wait_ge(rt_diff, 2 * l + 1)
                nc.scalar.activation(r4[:, 1], r4[:, 0], ACT.Exp).then_inc(rt_exp, 1)
                act.wait_ge(rt_diff, 2 * l + 2)
                nc.scalar.activation(rs[:, 5, :], rs[:, 4, :], ACT.Exp).then_inc(rt_exp, 1)
                act.wait_ge(routed, l + 1)
                with act.Fori(0, SETS) as g:
                    n = act.snap(g * ROUNDS + l * R_ALL)
                    most = act.value_load(cnt[0:1, bass.ds(g, 1)], min_val=0, max_val=SEQ)
                    expert_round(True, n)
                    with act.If(most > SLOTS):
                        with act.Fori(1, ROUNDS) as r:
                            with act.If(most > r * SLOTS):
                                m = act.snap(n + r)
                                expert_round(False, m)
                            with act.Else():
                                act.drain()
                                for s in (hg_a, gate_exp, y_a):
                                    act.sem_inc(s, 1)
                    with act.Else():
                        act.drain()
                        for s in (hg_a, gate_exp, y_a):
                            act.sem_inc(s, ROUNDS - 1)

        @block.vector
        def _(dve):
            V = nc.vector
            gap = dve.drain

            def hT_half(n):
                for t in range(TT):
                    dve.wait_ge(hT_ps, n * 2 * TT + 2 * t + 1)
                    V.tensor_copy(hT[:, 0:4, t * P:(t + 1) * P],
                                  ps[2 * t][:, :].rearrange("p (k c) -> p k c", k=4)).then_inc(hT_d, 1)

            def qk_norm(l, i):
                b = stage[:, i, :, :]
                rows = b.rearrange("p t c -> p (t c)")
                heads = rows.rearrange("p (h c) -> p h c", c=HD)
                dve.wait_ge(proj_out, l * 12 + 2 * i + 2)
                V.tensor_tensor(sq, rows, rows, ALU.mult)
                gap()
                V.tensor_reduce(hss[:, i * 16:i * 16 + 16], sq.rearrange("p (h c) -> p h c", c=HD),
                                AX.X, ALU.add).then_inc(qk_ss, 1)
                dve.wait_ge(qk_r, l * 2 + i + 1)
                V.tensor_tensor(heads, heads, hr[:, i * 16:i * 16 + 16].unsqueeze(2).broadcast_to([P, 16, HD]), ALU.mult)
                gap()
                V.tensor_tensor(heads, heads, over(qkg[:, i, :], 16), ALU.mult)
                gap()
                for t in range(TT):
                    h = b[:, t, :].rearrange("p (h c) -> p h c", c=HD)
                    first, second = h[:, :, 0:ROPE], h[:, :, ROPE:2 * ROPE]
                    cos = over(cst[:, C_COS + t * ROPE:C_COS + (t + 1) * ROPE], 8)
                    sin = over(cst[:, C_SIN + t * ROPE:C_SIN + (t + 1) * ROPE], 8)
                    part = [rope[:, n, t * 8 * ROPE:(t + 1) * 8 * ROPE].rearrange("p (h c) -> p h c", c=ROPE) for n in range(4)]
                    V.tensor_tensor(part[0], first, cos, ALU.mult)
                    V.tensor_tensor(part[1], second, sin, ALU.mult)
                    V.tensor_tensor(part[2], second, cos, ALU.mult)
                    V.tensor_tensor(part[3], first, sin, ALU.mult)
                gap()
                for t in range(TT):
                    h = b[:, t, :].rearrange("p (h c) -> p h c", c=HD)
                    part = [rope[:, n, t * 8 * ROPE:(t + 1) * 8 * ROPE].rearrange("p (h c) -> p h c", c=ROPE) for n in range(4)]
                    V.tensor_tensor(h[:, :, 0:ROPE], part[0], part[1], ALU.subtract)
                    last = V.tensor_tensor(h[:, :, ROPE:2 * ROPE], part[2], part[3], ALU.add)
                gap().then_inc(qk_normed, 1)

            def qkT_half(l, i):
                dve.wait_ge(qkT_ps, l * 8 + 2 * i + 1)
                V.tensor_copy(qk[:, i, :, 0:P], ps[2 * (i % 2)][:, :].rearrange("p (a c) -> p a c", a=PAIRS))\
                 .then_inc(qkT_d, 1)

            def da_scores(l, u):
                keys = P if u == 0 else 2 * P
                heads = HALF // keys
                mask = cst[:, C_MQ + (P if u == 0 else 0):C_MQ + 2 * P]
                dve.wait_ge(da_ps, l * 3 + u + 1)
                for e in range(2):
                    V.scalar_tensor_tensor(s_da[:, u, e, :].rearrange("p (h c) -> p h c", h=heads),
                                           ps[DAS_BANK[u][e]][:, :].rearrange("p (h c) -> p h c", h=heads),
                                           SCALE, over(mask, heads), ALU.mult, ALU.add)
                gap()
                V.tensor_reduce(dmax[:, u, 0:2 * heads], s_da[:, u].rearrange("p e (h c) -> p (e h) c", h=heads),
                                AX.X, ALU.max, negate=True).then_inc(da_max, 1)

            def da_mix_(l, u):
                keys = P if u == 0 else 2 * P
                heads = HALF // keys
                dve.wait_ge(da_exp, l * 3 + u + 1)
                V.reciprocal(dsum[:, u, 0:2 * heads], dsum[:, u, 0:2 * heads])
                gap()
                V.tensor_scalar(dsum[:, u, heads:2 * heads], dsum[:, u, heads:2 * heads], lams[:, 0:1], None, ALU.mult)
                gap()
                for h in range(heads):
                    c = slice(h * keys, (h + 1) * keys)
                    V.tensor_scalar(s_da[:, u, 0, c], s_da[:, u, 0, c], dsum[:, u, h:h + 1], None, ALU.mult)
                gap()
                for h in range(heads):
                    c = slice(h * keys, (h + 1) * keys)
                    V.scalar_tensor_tensor(s_da[:, u, 0, c], s_da[:, u, 1, c], dsum[:, u, heads + h:heads + h + 1],
                                           s_da[:, u, 0, c], ALU.mult, ALU.add)
                gap().then_inc(da_mix, 1)

            def sb_scores(l, ws):
                for w in ws:
                    heads = 4 if w >= 4 else 2
                    mask = cst[:, C_MS:C_MS + (P if w >= 4 else 2 * P)]
                    dve.wait_ge(sb_ps, l * 6 + SB_ORDER.index(w) + 1)
                    V.scalar_tensor_tensor(zm[:, w, :].rearrange("p (h c) -> p h c", h=heads),
                                           ps[SB_BANK[w]][:, :].rearrange("p (h c) -> p h c", h=heads),
                                           SCALE, over(mask, heads), ALU.mult, ALU.add)
                gap()
                for w in ws:
                    V.scalar_tensor_tensor(sp[:, w, :], zm[:, w, :], -1.0, zm[:, w, :], ALU.mult, ALU.min).then_inc(sb_abs, 1)

            def sb_softplus(l, ws):
                for w in ws:
                    dve.wait_ge(sb_ln, l * 6 + SB_ORDER.index(w) + 1)
                    V.scalar_tensor_tensor(sp[:, w, :], zm[:, w, :], 0.0, sp[:, w, :], ALU.max, ALU.add).then_inc(sb_sp, 1)

            def sb_argument(l, w):
                dve.wait_ge(sb_cum, l * 6 + SB_ORDER.index(w) + 1)
                V.tensor_tensor(zm[:, w, :], zm[:, w, :], ps[SB_BANK[w]][:, :], ALU.subtract).then_inc(sb_arg, 1)

            def first_of(onehot, values, top, weights):
                V.tensor_tensor(onehot, values, top.unsqueeze(2).broadcast_to(list(values.shape)), ALU.is_equal)
                gap()
                V.tensor_tensor(onehot, onehot, over(weights, TT), ALU.mult)
                gap()
                V.tensor_reduce(rs[:, 7, :], onehot, AX.X, ALU.max)
                gap()
                V.tensor_tensor(onehot, onehot, rs[:, 7, :].unsqueeze(2).broadcast_to(list(values.shape)), ALU.is_equal)
                gap()

            def select(n):
                shape = [P, LANES, SLOTS]
                slot = cst[:, C_IOTA:C_REV].rearrange("p (j s) -> p j s", j=LANES)
                for t in range(TT):
                    V.tensor_tensor(sel[:, t, :].rearrange("p (j s) -> p j s", j=LANES), slot,
                                    posg[:, t, :].unsqueeze(2).broadcast_to(shape), ALU.is_equal)
                gap()
                for t in range(TT):
                    V.tensor_tensor(selw[:, t, :].rearrange("p (j s) -> p j s", j=LANES),
                                    sel[:, t, :].rearrange("p (j s) -> p j s", j=LANES),
                                    wgg[:, t, :].unsqueeze(2).broadcast_to(shape), ALU.mult)
                gap().then_inc(sel_ready, 1)

            def expert_round(n):
                select(n)
                dve.wait_ge(gathered, n + 1)
                V.tensor_copy(hgT[:, 0:4, :], ps[0][:, :].rearrange("p (k s) -> p k s", k=4)).then_inc(hg_d, 1)
                dve.wait_ge(selwT_ps, n + 1)
                V.tensor_copy(selwT.rearrange("p t s -> p (t s)"), ps[3][:, 0:TT * P]).then_inc(selwT_out, 1)
                dve.wait_ge(gate_exp, n + 1)
                V.tensor_scalar(rg, eg, 1.0, None, ALU.add)
                gap()
                V.reciprocal(rg, rg)
                gap()
                V.tensor_tensor(tg, ps[2][:, 0:FF], rg, ALU.mult)
                gap()
                V.tensor_tensor(act_sb.rearrange("p (c f) -> p f c", c=FC),
                                ps[2][:, FF:2 * FF].rearrange("p (f c) -> p f c", c=FC),
                                tg.rearrange("p (f c) -> p f c", c=FC), ALU.mult).then_inc(act_out, 1)
                dve.wait_ge(actT_ps, n + 1)
                V.tensor_copy(actT.rearrange("p c s -> p (c s)"), ps[3][:, 0:FF]).then_inc(actT_out, 1)
                dve.wait_ge(dn_ps, n + 1)
                V.tensor_copy(y[:, 0:HALF], ps[4][:, :]).then_inc(y_d, 1)
                dve.wait_ge(sc_ps, n + 1)
                for t in range(TT):
                    for h in range(2):
                        c = slice(h * HALF, (h + 1) * HALF)
                        V.tensor_tensor(x_sb[:, t, c], x_sb[:, t, c], ps[SC_BANK[t][h]][:, :], ALU.add)
                gap().then_inc(x_moe, 1)

            dve.wait_ge(const_in, 16)
            for l in range(DEPTH):
                lam_init = 0.8 - 0.6 * math.exp(-0.3 * l)
                dve.wait_ge(par_in, (l + 1) * N_PAR)
                if l == 0:
                    dve.wait_ge(x_in, 16)
                dve.wait_ge(norm_r, 2 * l + 1)
                for t in range(TT):
                    V.scalar_tensor_tensor(xn[:, t, :], x_sb[:, t, :], rstd[:, t:t + 1], g1[:, :],
                                           ALU.mult, ALU.mult).then_inc(h_ready, 1)
                prod = sq[:, 0:2 * HD].rearrange("p (n c) -> p n c", n=2)
                V.tensor_tensor(prod, lamv[:, 0:4:2, :], lamv[:, 1:4:2, :], ALU.mult)
                gap()
                V.tensor_reduce(lams[:, 0:2], prod, AX.X, ALU.add).then_inc(lam_dot, 1)
                hT_half(2 * l)
                dve.wait_ge(lam_exp, l + 1)
                V.tensor_scalar(lams[:, 0:1], lams[:, 3:4], lams[:, 2:3], -lam_init, ALU.subtract, ALU.add)
                gap()
                qk_norm(l, 0)
                qk_norm(l, 1)
                for i in range(4):
                    qkT_half(l, i)
                da_scores(l, 0)
                da_scores(l, 1)
                da_mix_(l, 0)
                da_mix_(l, 1)
                da_scores(l, 2)
                dve.wait_ge(proj_out, l * 12 + 12)
                sb_scores(l, (4, 5))
                da_mix_(l, 2)
                sb_scores(l, (0, 1))
                sb_softplus(l, (4, 5))
                sb_scores(l, (2, 3))
                sb_softplus(l, (0, 1))
                sb_argument(l, 4)
                sb_argument(l, 5)
                sb_softplus(l, (2, 3))
                for w in range(4):
                    sb_argument(l, w)
                dve.wait_ge(o_sq, l + 1)
                V.tensor_reduce(oss[:, 0, 0:8], osq[:, 0:2, :].rearrange("p u (h c) -> p (u h) c", c=2 * HD), AX.X, ALU.add)
                V.tensor_reduce(hss[:, 0:16], osq[:, 2:4, :].rearrange("p u (h c) -> p (u h) c", c=HD), AX.X, ALU.add)
                gap().then_inc(o_ss, 1)
                dve.wait_ge(o_r, l + 1)
                for t in range(TT):
                    V.tensor_tensor(xn[:, t, 0:HALF].rearrange("p (h c) -> p h c", c=2 * HD),
                                    ps[DAO_BANK[t]][:, :].rearrange("p (h c) -> p h c", c=2 * HD),
                                    oss[:, 1, 4 * t:4 * t + 4].unsqueeze(2).broadcast_to([P, 4, 2 * HD]), ALU.mult)
                    V.tensor_tensor(xn[:, t, HALF:].rearrange("p (h c) -> p h c", c=HD),
                                    ps[SBO_BANK[t]][:, :].rearrange("p (h c) -> p h c", c=HD),
                                    hr[:, 8 * t:8 * t + 8].unsqueeze(2).broadcast_to([P, 8, HD]), ALU.mult)
                gap()
                for t in range(TT):
                    o = xn[:, t, 0:HALF].rearrange("p (h c) -> p h c", c=2 * HD)
                    V.scalar_tensor_tensor(o, o, 1.0 - lam_init, over(dag[:, :], 4), ALU.mult, ALU.mult)
                    o = xn[:, t, HALF:].rearrange("p (h c) -> p h c", c=HD)
                    V.tensor_tensor(o, o, over(sbg[:, :], 8), ALU.mult)
                gap().then_inc(o_ready, 1)
                for t in range(TT):
                    dve.wait_ge(oT_ps, l * 4 + 2 * t + 1)
                    V.tensor_copy(hT[:, 0:4, t * P:(t + 1) * P],
                                  ps[OT_BANK[t][0]][:, :].rearrange("p (k c) -> p k c", k=4)).then_inc(oT_d, 1)
                for h in range(2):
                    for t in range(TT):
                        dve.wait_ge(oproj_ps, l * 4 + 2 * h + t + 1)
                        c = slice(h * HALF, (h + 1) * HALF)
                        V.tensor_tensor(x_sb[:, t, c], x_sb[:, t, c], ps[OP_BANK[h][t]][:, :], ALU.add).then_inc(x_attn, 1)
                dve.wait_ge(norm_r, 2 * l + 2)
                for t in range(TT):
                    V.scalar_tensor_tensor(xn[:, t, :].rearrange("p (k c) -> p c k", k=KC),
                                           x_sb[:, t, :].rearrange("p (c k) -> p c k", k=KC), rstd[:, t:t + 1],
                                           g2[:, :].rearrange("p (c k) -> p c k", k=KC),
                                           ALU.mult, ALU.mult).then_inc(h_ready, 1)
                hT_half(2 * l + 1)
                dve.wait_ge(lg_ps, l + 1)
                V.tensor_tensor(lg[:, :, :], ps[4][:, 0:2 * 64].rearrange("p (t n) -> p t n", t=TT)[:, :, 0:GROUPS + EXPERTS],
                                over(br[:, :], TT), ALU.add)
                gap()
                gl, el = lg[:, :, 0:GROUPS], lg[:, :, GROUPS:]
                V.tensor_reduce(rs[:, 0, :], gl, AX.X, ALU.max)
                gap()
                V.tensor_tensor(r4[:, 0], gl, rs[:, 0, :].unsqueeze(2).broadcast_to([P, TT, GROUPS]), ALU.subtract).then_inc(rt_diff, 1)
                first_of(r4[:, 2], gl, rs[:, 0, :], cst[:, C_REV:C_REV + GROUPS])
                V.tensor_scalar(r4[:, 3], r4[:, 2], -NEG, NEG, ALU.mult, ALU.add)
                gap()
                for t in range(TT):
                    V.tensor_tensor(em[:, t, :].rearrange("p (g e) -> p g e", g=GROUPS),
                                    el[:, t, :].rearrange("p (g e) -> p g e", g=GROUPS),
                                    r4[:, 3, t, :].unsqueeze(2).broadcast_to([P, GROUPS, PER_GROUP]), ALU.add)
                gap()
                V.tensor_reduce(rs[:, 1, :], em[:, :, :], AX.X, ALU.max)
                gap()
                first_of(oh1[:, :, :], em[:, :, :], rs[:, 1, :], cst[:, C_REV:C_COS])
                V.scalar_tensor_tensor(ev[:, :, :], oh1[:, :, :], 3 * NEG, em[:, :, :], ALU.mult, ALU.add)
                gap()
                V.tensor_reduce(rs[:, 2, :], ev[:, :, :], AX.X, ALU.max)
                gap()
                V.tensor_tensor(rs[:, 4, :], rs[:, 2, :], rs[:, 1, :], ALU.subtract).then_inc(rt_diff, 1)
                first_of(oh2[:, :, :], ev[:, :, :], rs[:, 2, :], cst[:, C_REV:C_COS])
                V.tensor_tensor(asg[:, :, :], oh1[:, :, :], oh2[:, :, :], ALU.add).then_inc(rt_asg, 1)
                dve.wait_ge(rt_exp, 2 * l + 2)
                V.tensor_reduce(rs[:, 3, :], r4[:, 1], AX.X, ALU.add)
                V.tensor_scalar(rs[:, 6, :], rs[:, 5, :], 1.0, None, ALU.add)
                gap()
                V.tensor_tensor(rs[:, 3, :], rs[:, 3, :], rs[:, 6, :], ALU.mult)
                gap()
                V.reciprocal(rs[:, 3, :], rs[:, 3, :])
                gap()
                V.tensor_tensor(rs[:, 6, :], rs[:, 3, :], rs[:, 5, :], ALU.mult)
                gap()
                for t in range(TT):
                    V.tensor_scalar(wgt[:, t, :], oh1[:, t, :], rs[:, 3, t:t + 1], None, ALU.mult)
                gap()
                for t in range(TT):
                    V.scalar_tensor_tensor(wgt[:, t, :], oh2[:, t, :], rs[:, 6, t:t + 1], wgt[:, t, :], ALU.mult, ALU.add)
                dve.wait_ge(pos_ps, l + 1)
                V.scalar_tensor_tensor(pos[:, :, :], ps[5][:, 0:2 * EXPERTS].rearrange("p (t e) -> p t e", t=TT), 1.0,
                                       asg[:, :, :], ALU.add, ALU.mult)
                V.tensor_reduce(cntf[:, :], ps[5][:, 2 * EXPERTS:3 * EXPERTS].rearrange("p (g j) -> p g j", j=LANES), AX.X, ALU.max)
                gap()
                V.tensor_scalar(pos[:, :, :], pos[:, :, :], -1.0, None, ALU.add)
                V.tensor_copy(cnt[:, :], cntf[:, :])
                gap().then_inc(routed, 1)
                with dve.Fori(0, SETS) as g:
                    n = dve.snap(g * ROUNDS + l * R_ALL)
                    most = dve.value_load(cnt[0:1, bass.ds(g, 1)], min_val=0, max_val=SEQ)
                    for t in range(TT):
                        V.tensor_copy(posg[:, t, :], pos[:, t, bass.ds(g * LANES, LANES)])
                        V.tensor_copy(wgg[:, t, :], wgt[:, t, bass.ds(g * LANES, LANES)])
                    gap()
                    expert_round(n)
                    with dve.If(most > SLOTS):
                        with dve.Fori(1, ROUNDS) as r:
                            with dve.If(most > r * SLOTS):
                                m = dve.snap(n + r)
                                V.tensor_scalar(posg[:, :, :], posg[:, :, :], -float(SLOTS), None, ALU.add)
                                gap()
                                expert_round(m)
                            with dve.Else():
                                gap()
                                for s in DVE_ROUND:
                                    dve.sem_inc(s, 1)
                    with dve.Else():
                        gap()
                        for s in DVE_ROUND:
                            dve.sem_inc(s, ROUNDS - 1)

        @block.tensor
        def _(pe):
            MM, TR = nc.tensor.matmul, nc.tensor.transpose

            def transpose_x(n):
                for t in range(TT):
                    pe.wait_ge(h_ready, n * TT + t + 1)
                    for k in range(KC):
                        last = TR(ps[2 * t + k // 4][:, (k % 4) * P:(k % 4 + 1) * P], xn[:, t, k * P:(k + 1) * P], ident)
                        if k % 4 == 3:
                            last.then_inc(hT_ps, 1)

            def proj(l, i):
                n = l * XUNITS + i
                pe.wait_ge(xslot_in[i % 2], (n // 2 + 1) * 16)
                for t in range(TT):
                    if i == 0:
                        pe.wait_ge(hT_d, 2 * l * TT + t + 1)
                        pe.wait_ge(hT_a, 2 * l * TT + t + 1)
                    if i >= 2:
                        pe.wait_ge(proj_out, l * 12 + 2 * (i - 2) + t + 1)
                    for k in range(KC):
                        last = MM(ps[4 + (2 * i + t) % 4][:, :], hT[:, k, t * P:(t + 1) * P], xbuf[:, i % 2, k, :],
                                  start=(k == 0), stop=(k == KC - 1))
                    last.then_inc(proj_ps, 1)
                pe.drain().then_inc(xslot_used, 1)

            def transpose_qk(l, i):
                if i < 2:
                    pe.wait_ge(qk_normed, l * 2 + i + 1)
                else:
                    pe.wait_ge(proj_out, l * 12 + 2 * i + 2)
                if i == 0:
                    pe.wait_ge(hT_a, 2 * l * TT + TT)
                    pe.wait_ge(hT_d, 2 * l * TT + TT)
                if i >= 2:
                    pe.wait_ge(qkT_d, l * 4 + i - 1)
                    pe.wait_ge(qkT_a, l * 4 + i - 1)
                for t in range(TT):
                    for a in range(PAIRS):
                        last = TR(ps[2 * (i % 2) + t][:, a * P:(a + 1) * P], stage[:, i % 2, t, a * P:(a + 1) * P], ident)
                    last.then_inc(qkT_ps, 1)

            def da_scores(l, u):
                keys = P if u == 0 else 2 * P
                heads = HALF // keys
                q0 = 0 if u == 0 else P
                a0 = 2 if u == 2 else 0
                for h in range(heads):
                    for e in range(2):
                        rows = slice(e * HD, (e + 1) * HD)
                        last = MM(ps[DAS_BANK[u][e]][:, h * keys:(h + 1) * keys], qk[rows, 0, a0 + h, q0:q0 + P],
                                  qk[rows, 1, a0 + h, 0:keys], start=True, stop=True)
                pe.drain().then_inc(da_ps, 1)

            def sb_scores(l, we, wo):
                kt = 1 if we >= 4 else 0
                heads = 4 if kt else 2
                a0 = we if not kt else 0
                for h in range(heads):
                    for e, w in enumerate((we, wo)):
                        rows = slice(e * HD, (e + 1) * HD)
                        n = SEQ - kt * P
                        MM(ps[SB_BANK[w]][:, h * n:(h + 1) * n], qk[rows, 3, a0 + h, kt * P:(kt + 1) * P],
                           qk[rows, 2, a0 + h, kt * P:SEQ], start=True, stop=True)
                pe.drain().then_inc(sb_ps, 2)

            def da_transpose(l, u):
                pe.wait_ge(da_mix, l * 3 + u + 1)
                for b in range(4):
                    last = TR(ps[DAT_BANK[u]][:, b * P:(b + 1) * P], s_da[:, u, 0, b * P:(b + 1) * P], ident)
                last.then_inc(daT_ps, 1)

            def cumulate(l, w):
                pe.wait_ge(sb_sp, l * 6 + SB_ORDER.index(w) + 1)
                MM(ps[SB_BANK[w]][:, :], tri_ge, sp[:, w, :], start=True, stop=(w >= 4))
                if w < 4:
                    MM(ps[SB_BANK[w]][:, :].rearrange("p (h q) -> p h q", h=2)[:, :, P:], ones,
                       sp[:, 4 + w % 2, (w // 2) * 2 * P:(w // 2 + 1) * 2 * P].rearrange("p (h q) -> p h q", h=2),
                       start=False, stop=True)
                pe.drain().then_inc(sb_cum, 1)

            def router(l):
                pe.wait_ge(hT_d, (2 * l + 1) * TT + TT)
                pe.wait_ge(hT_a, (2 * l + 1) * TT + TT)
                for t in range(TT):
                    for k in range(KC):
                        last = MM(ps[4][:, t * 64:t * 64 + GROUPS + EXPERTS], hT[:, k, t * P:(t + 1) * P], wr[:, k, :],
                                  start=(k == 0), stop=(k == KC - 1))
                last.then_inc(lg_ps, 1)
                pe.wait_ge(rt_asg, l + 1)
                MM(ps[5][:, 0:EXPERTS], tri_lt, asg[:, 0, :], start=True, stop=True)
                MM(ps[5][:, EXPERTS:2 * EXPERTS], ones, asg[:, 0, :], start=True, stop=False)
                MM(ps[5][:, EXPERTS:2 * EXPERTS], tri_lt, asg[:, 1, :], start=False, stop=True)
                MM(ps[5][:, 2 * EXPERTS:3 * EXPERTS], ones, asg[:, 0, :], start=True, stop=False)
                MM(ps[5][:, 2 * EXPERTS:3 * EXPERTS], ones, asg[:, 1, :], start=False, stop=True).then_inc(pos_ps, 1)

            def gather_up(n):
                pe.wait_ge(sel_ready, n + 1)
                for k in range(KC):
                    for t in range(TT):
                        last = MM(ps[k // 4][:, (k % 4) * P:(k % 4 + 1) * P], xn[:, t, k * P:(k + 1) * P], sel[:, t, :],
                                  start=(t == 0), stop=(t == TT - 1))
                last.then_inc(gathered, 1)
                for t in range(TT):
                    last = TR(ps[3][:, t * P:(t + 1) * P], selw[:, t, :], ident)
                last.then_inc(selwT_ps, 1)
                pe.wait_ge(hg_d, n + 1)
                pe.wait_ge(hg_a, n + 1)
                for k in range(KC):
                    for j in range(LANES):
                        last = MM(ps[2][j * SLOTS:(j + 1) * SLOTS, :], hgT[:, k, j * SLOTS:(j + 1) * SLOTS],
                                  gubuf[:, j, k, :, :].rearrange("p a f -> p (a f)"),
                                  start=(k == 0), stop=(k == KC - 1))
                pe.drain().then_inc(gu_ps, 1)

            def down_scatter(n, wait_down):
                pe.wait_ge(act_out, n + 1)
                pe.wait_ge(selwT_out, n + 1)
                for c in range(FC):
                    last = TR(ps[3][:, c * P:(c + 1) * P], act_sb[:, c * P:(c + 1) * P], ident)
                last.then_inc(actT_ps, 1)
                wait_down()
                pe.wait_ge(actT_out, n + 1)
                for c in range(FC):
                    for h in range(2):
                        for j in range(LANES):
                            MM(ps[4 + h][j * SLOTS:(j + 1) * SLOTS, :], actT[:, c, j * SLOTS:(j + 1) * SLOTS],
                               dnbuf[:, j, c * D + h * HALF:c * D + (h + 1) * HALF], start=(c == 0), stop=(c == FC - 1))
                pe.drain().then_inc(dn_ps, 1)
                pe.wait_ge(y_d, n + 1)
                pe.wait_ge(y_a, n + 1)
                for t in range(TT):
                    for h in range(2):
                        last = MM(ps[SC_BANK[t][h]][:, :], selwT[:, t, :], y[:, h * HALF:(h + 1) * HALF], start=True, stop=True)
                last.then_inc(sc_ps, 1)
                pe.wait_ge(x_moe, n + 1)

            pe.wait_ge(const_in, 16)
            for l in range(DEPTH):
                transpose_x(2 * l)
                proj(l, 0)
                proj(l, 1)
                transpose_qk(l, 0)
                proj(l, 2)
                transpose_qk(l, 1)
                proj(l, 3)
                transpose_qk(l, 2)
                transpose_qk(l, 3)
                pe.wait_ge(qkT_d, l * 4 + 4)
                pe.wait_ge(qkT_a, l * 4 + 4)
                da_scores(l, 0)
                da_scores(l, 1)
                proj(l, 4)
                pe.wait_ge(da_max, l * 3 + 1)
                da_scores(l, 2)
                proj(l, 5)
                pe.wait_ge(da_max, l * 3 + 2)
                sb_scores(l, 4, 5)
                pe.wait_ge(proj_out, l * 12 + 10)
                sb_scores(l, 0, 1)
                pe.wait_ge(da_max, l * 3 + 3)
                sb_scores(l, 2, 3)
                pe.wait_ge(proj_out, l * 12 + 12)
                da_transpose(l, 0)
                da_transpose(l, 1)
                cumulate(l, 4)
                cumulate(l, 5)
                pe.wait_ge(daT_out, l * 3 + 1)
                da_transpose(l, 2)
                cumulate(l, 0)
                cumulate(l, 1)
                cumulate(l, 2)
                cumulate(l, 3)
                pe.wait_ge(daT_out, l * 3 + 3)
                for a in range(PAIRS):
                    MM(ps[DAO_BANK[0]][:, a * P:(a + 1) * P], aT[:, 0, a, :], v_sb[:, 0, 0, a * P:(a + 1) * P],
                       start=True, stop=True)
                for a in range(PAIRS):
                    for kt in range(TT):
                        last = MM(ps[DAO_BANK[1]][:, a * P:(a + 1) * P], aT[:, 1 + a // 2, 2 * (a % 2) + kt, :],
                                  v_sb[:, kt, 0, a * P:(a + 1) * P], start=(kt == 0), stop=(kt == TT - 1))
                last.then_inc(da_o, 1)
                pe.wait_ge(sb_a, l * 6 + 6)
                for hh in range(2 * PAIRS):
                    a, e = hh // 2, hh % 2
                    early = zm[:, 2 * (a // 2) + e, (a % 2) * SEQ:(a % 2 + 1) * SEQ]
                    late = zm[:, 4 + e, a * P:(a + 1) * P]
                    cols = slice(hh * HD, (hh + 1) * HD)
                    MM(ps[SBO_BANK[0]][:, cols], early[:, 0:P], v_sb[:, 0, 1, cols], start=True, stop=True)
                    MM(ps[SBO_BANK[1]][:, cols], early[:, P:SEQ], v_sb[:, 0, 1, cols], start=True, stop=False)
                    last = MM(ps[SBO_BANK[1]][:, cols], late, v_sb[:, 1, 1, cols], start=False, stop=True)
                last.then_inc(sb_o, 1)
                pe.wait_ge(o_ready, l + 1)
                for t in range(TT):
                    for k in range(KC):
                        last = TR(ps[OT_BANK[t][k // 4]][:, (k % 4) * P:(k % 4 + 1) * P], xn[:, t, k * P:(k + 1) * P], ident)
                        if k % 4 == 3:
                            last.then_inc(oT_ps, 1)
                pe.wait_ge(oT_d, l * 2 + 2)
                pe.wait_ge(oT_a, l * 2 + 2)
                for h in range(2):
                    i = len(ORDER) + h
                    pe.wait_ge(xslot_in[i % 2], ((l * XUNITS + i) // 2 + 1) * 16)
                    for t in range(TT):
                        for k in range(KC):
                            last = MM(ps[OP_BANK[h][t]][:, :], hT[:, k, t * P:(t + 1) * P], xbuf[:, i % 2, k, :],
                                      start=(k == 0), stop=(k == KC - 1))
                        last.then_inc(oproj_ps, 1)
                    pe.drain().then_inc(xslot_used, 1)
                transpose_x(2 * l + 1)
                router(l)
                pe.wait_ge(routed, l + 1)
                with pe.Fori(0, SETS) as g:
                    n = pe.snap(g * ROUNDS + l * R_ALL)
                    most = pe.value_load(cnt[0:1, bass.ds(g, 1)], min_val=0, max_val=SEQ)
                    for j in range(LANES):
                        pe.wait_ge(gu_in[j], g * 32 + (l * SETS + 1) * 32)
                    gather_up(n)
                    with pe.If(most <= SLOTS):
                        pe.sem_inc(gu_used, 1)

                    def wait_down():
                        for j in range(LANES):
                            pe.wait_ge(dn_in[j], g * 16 + (l * SETS + 1) * 16)
                    down_scatter(n, wait_down)
                    with pe.If(most > SLOTS):
                        with pe.Fori(1, ROUNDS) as r:
                            with pe.If(most > r * SLOTS):
                                m = pe.snap(n + r)
                                gather_up(m)
                                down_scatter(m, lambda: None)
                            with pe.Else():
                                pe.drain()
                                for s in PE_ROUND:
                                    pe.sem_inc(s, 1)
                        pe.sem_inc(gu_used, 1)
                    with pe.Else():
                        pe.drain()
                        for s in PE_ROUND:
                            pe.sem_inc(s, ROUNDS - 1)
                    pe.sem_inc(dn_used, 1)


NAMES = ["x", "norm1_g", "w_in", "q_norm_g", "k_norm_g", "lambda_q1", "lambda_k1", "lambda_q2", "lambda_k2",
         "da_out_g", "sb_out_g", "w_out", "norm2_g", "w_router_group", "b_router_group", "w_router_expert",
         "b_router_expert", "w_gate", "w_up", "w_down"]


def kernel(**inputs):
    import concourse.bacc as bacc
    from concourse.bass_utils import run_bass_kernel_spmd

    nc = bacc.Bacc("TRN2", target_bir_lowering=False, num_devices=1)
    arrays = {"in_const": shape_constants()}
    arrays |= {f"in_{n}": np.ascontiguousarray(inputs[n]) for n in NAMES}
    aps = [nc.dram_tensor(n, a.shape, mybir.dt.from_np(a.dtype), kind="ExternalInput").ap() for n, a in arrays.items()]
    out = nc.dram_tensor("out_0", (1, SEQ, D), F32, kind="ExternalOutput").ap()
    decoder(nc, *aps, out)
    return run_bass_kernel_spmd(nc, [arrays], core_ids=[0]).results[0]["out_0"]
```

```python
import math
from contextlib import ExitStack

import concourse.bass as bass
import numpy as np
from concourse import mybir

F32 = mybir.dt.float32
I32 = mybir.dt.int32
ALU = mybir.AluOpType
ACT = mybir.ActivationFunctionType
AX = mybir.AxisListType

P = 128
D = 1024
SEQ = 256
DEPTH = 2
TT = SEQ // P
KC = D // P
HD = 64
PAIRS = 4
HALF = D // 2
GROUPS, PER_GROUP, EXPERTS = 4, 8, 32
FF = D // 4
FC = FF // P
LANES = 4
SLOTS = P // LANES
ROUNDS = SEQ // SLOTS
SETS = EXPERTS // LANES
ROPE = HD // 8
ROPE_THETA = 500000.0
EPS = 1e-6
SCALE = HD ** -0.5
NEG = -1e30
BIG = 64.0

DA_Q, DA_K, DA_V, SB_Q, SB_K, SB_V = range(6)
ORDER = [DA_Q, DA_K, SB_Q, SB_K, DA_V, SB_V]
BLOCKS = len(ORDER) + 2
SLOTS_W = 6
UNITS = BLOCKS + EXPERTS


def block_slot(l, i):
    a, b = ((0, 1), (4, 5)) if l % 2 == 0 else ((4, 5), (0, 1))
    return (a + b + (2, 3) + a)[i]


def lane_slot(l, g, j):
    return block_slot(l, 2 + j - 2 * (g % 2)) if j < 2 else j



SB_ORDER = [4, 5, 0, 1, 2, 3]
PROJ_BANK = [(4, 5), (6, 7), (4, 5), (6, 7), (4, 5), (4, 5)]
QKT_BANK = [(0, 1), (2, 3), (2, 3), (0, 1)]
DAS_BANK = [(0, 1), (2, 3), (0, 1)]
DAT_BANK = [6, 7, 6]
SB_BANK = [0, 1, 6, 7, 2, 3]
DAO_BANK = [2, 3]
SBO_BANK = [4, 5]
OT_BANK = [(0, 1), (6, 7)]
OP_BANK = [(2, 4), (3, 5)]
SC_BANK = [(6, 7), (4, 5)]

C_ID, C_GE, C_LT, C_ONE, C_MQ, C_MS, C_IOTA, C_REV, C_OFF, C_COS, C_SIN, C_END = np.cumsum(
    [0, P, P, P, P, 2 * P, 2 * P, P, EXPERTS, ROUNDS, TT * ROPE, TT * ROPE]).tolist()


def shape_constants():
    c = np.zeros((P, C_END), np.float32)
    i = np.arange(P)
    c[:, C_ID:C_GE] = np.eye(P)
    c[:, C_GE:C_LT] = i[:, None] >= i[None, :]
    c[:, C_LT:C_ONE] = i[:, None] < i[None, :]
    c[:, C_ONE:C_MQ] = 1.0
    c[:, C_MQ + P:C_MS] = np.where(i[None, :] <= i[:, None], 0.0, NEG)
    c[:, C_MS:C_MS + P] = np.where(i[:, None] < i[None, :], 0.0, NEG)
    c[:, C_IOTA:C_REV] = i % SLOTS
    c[:, C_REV:C_OFF] = BIG - np.arange(EXPERTS)
    c[:, C_OFF:C_COS] = SLOTS * np.arange(ROUNDS)
    freq = (1.0 / (np.float32(ROPE_THETA) ** (np.arange(0, 2 * ROPE, 2, dtype=np.float32) / (2 * ROPE))))
    angle = np.arange(SEQ, dtype=np.float32)[:, None] * freq.astype(np.float32)[None, :]
    angle = angle.reshape(TT, P, ROPE).transpose(1, 0, 2).reshape(P, TT * ROPE).astype(np.float64)
    c[:, C_COS:C_SIN] = np.cos(angle)
    c[:, C_SIN:C_END] = np.sin(angle)
    return c


def decoder(nc, const, x, norm1_g, w_in, q_norm_g, k_norm_g, lambda_q1, lambda_k1, lambda_q2, lambda_k2,
            da_out_g, sb_out_g, w_out, norm2_g, w_router_group, b_router_group, w_router_expert,
            b_router_expert, w_gate, w_up, w_down, out):
    with ExitStack() as ctx:
        def sb(name, shape, dt=F32):
            return ctx.enter_context(nc.sbuf_tensor(name, shape, dt))

        def sem(name):
            return ctx.enter_context(nc.semaphore(name))

        wbuf = sb("wbuf", [P, SLOTS_W, KC * HALF])
        dnbuf = sb("dnbuf", [P, LANES, FC * D])
        x_sb = sb("x_sb", [P, TT, D])
        xn = sb("xn", [P, TT, D])
        work = sb("work", [P, 8 * HALF])
        qkT = sb("qkT", [P, 4 * PAIRS * SEQ])
        v_sb = sb("v_sb", [P, TT, 2, HALF])
        cst = sb("cst", [P, C_END])
        g1 = sb("g1", [P, D])
        g2 = sb("g2", [P, D])
        wr = sb("wr", [P, KC, GROUPS + EXPERTS])
        br = sb("br", [P, GROUPS + EXPERTS])
        qkg = sb("qkg", [P, 2, HD])
        dag = sb("dag", [P, 2 * HD])
        sbg = sb("sbg", [P, HD])
        lamv = sb("lamv", [P, 4, HD])
        lams = sb("lams", [P, 4])
        ssq = sb("ssq", [P, TT])
        rstd = sb("rstd", [P, TT])
        hss = sb("hss", [P, 2 * 16])
        hr = sb("hr", [P, 2 * 16])
        rope = sb("rope", [P, 4, TT * 8 * ROPE])
        dmax = sb("dmax", [P, 3, 8])
        dsum = sb("dsum", [P, 3, 8])
        oss = sb("oss", [P, TT, 24])
        lg = sb("lg", [P, TT, GROUPS + EXPERTS])
        rs = sb("rs", [P, 8, TT])
        r4 = sb("r4", [P, 4, TT, GROUPS])
        em = sb("em", [P, TT, EXPERTS])
        ev = sb("ev", [P, TT, EXPERTS])
        oh1 = sb("oh1", [P, TT, EXPERTS])
        oh2 = sb("oh2", [P, TT, EXPERTS])
        asg = sb("asg", [P, TT + 1, EXPERTS])
        wgt = sb("wgt", [P, TT, EXPERTS + LANES])
        pos = sb("pos", [P, TT, EXPERTS + LANES])
        posg = sb("posg", [P, TT, LANES])
        wgg = sb("wgg", [P, TT, LANES])
        cntf = sb("cntf", [P, SETS])
        cnt = sb("cnt", [P, SETS], I32)

        ident = cst[:, C_ID:C_GE]
        tri_ge = cst[:, C_GE:C_LT]
        tri_lt = cst[:, C_LT:C_ONE]
        ones = cst[:, C_ONE:C_MQ]

        def over(ap, n):
            return ap.unsqueeze(1).broadcast_to([P, n, ap.shape[1]])

        hT = work[:, 0:KC * SEQ].rearrange("p (k t) -> p k t", k=KC)
        stage = work[:, KC * SEQ:].rearrange("p (b t c) -> p b t c", b=2, t=TT)
        scratch = dnbuf[:, :, :].rearrange("p a b -> p (a b)")
        s_da = scratch[:, 0:6 * HALF].rearrange("p (u e c) -> p u e c", u=3, e=2)
        zm = scratch[:, 6 * HALF:12 * HALF].rearrange("p (u c) -> p u c", u=6)
        aT = [s_da[:, u, 1, :].rearrange("p (b c) -> p b c", b=4) for u in range(3)]
        sp = [xn[:, w // 2, (w % 2) * HALF:(w % 2 + 1) * HALF] for w in range(4)] + \
             [scratch[:, (12 + w) * HALF:(13 + w) * HALF] for w in range(2)]
        sq = scratch[:, 6 * HALF:8 * HALF]
        osq = scratch[:, 0:4 * HALF].rearrange("p (u c) -> p u c", u=4)
        qk = qkT[:, :].rearrange("p (i a t) -> p i a t", i=4, a=PAIRS)
        at = [0]

        def take(n):
            at[0] += n
            return qkT[:, at[0] - n:at[0]]
        hgT = take(KC * P).rearrange("p (k s) -> p k s", k=KC)
        y = take(D)
        eg, rg, tg = take(FF), take(FF), take(FF)
        act_sb = take(FF)
        actT = take(FF).rearrange("p (c s) -> p c s", c=FC)
        sel = take(TT * P).rearrange("p (t s) -> p t s", t=TT)
        selw = take(TT * P).rearrange("p (t s) -> p t s", t=TT)
        selwT2 = [take(TT * P).rearrange("p (t s) -> p t s", t=TT),
                  work[:, KC * P:KC * P + TT * P].rearrange("p (t s) -> p t s", t=TT)]
        hgT_more = work[:, 0:KC * P].rearrange("p (k s) -> p k s", k=KC)
        selwT_more = work[:, (KC + TT) * P:(KC + 2 * TT) * P].rearrange("p (t s) -> p t s", t=TT)

        ps = [ctx.enter_context(nc.psum_tensor(f"bank{i}", [P, HALF], F32)) for i in range(8)]

        ident_in, const_in = sem("ident_in"), sem("const_in")
        x_in = [sem(f"x_in{t}") for t in range(TT)]
        g1_in = [sem(f"g1_in{l}") for l in range(DEPTH)]
        par_in = [sem(f"par_in{l}") for l in range(DEPTH)]
        block_in = [sem(f"block_in{i}") for i in range(BLOCKS)]
        block0_rest_in = sem("block0_rest_in")
        gu_in = [sem(f"gu_in{j}") for j in range(LANES)]
        dn_in = [sem(f"dn_in{j}") for j in range(LANES)]
        out_done = sem("out_done")
        norm_r, h_ready = sem("norm_r"), sem("h_ready")
        hT_ps, hT_d, hT_a = sem("hT_ps"), sem("hT_d"), sem("hT_a")
        proj_ps, proj_out, slot_used = sem("proj_ps"), sem("proj_out"), sem("slot_used")
        qk_ss, qk_r, qk_normed = sem("qk_ss"), sem("qk_r"), sem("qk_normed")
        qkT_ps, qkT_d, qkT_a = sem("qkT_ps"), sem("qkT_d"), sem("qkT_a")
        lam_dot, lam_exp = sem("lam_dot"), sem("lam_exp")
        da_ps, da_max, da_exp, da_mix = sem("da_ps"), sem("da_max"), sem("da_exp"), sem("da_mix")
        daT_ps, daT_out, o_ps = sem("daT_ps"), sem("daT_out"), sem("o_ps")
        sb_ps, sb_abs, sb_ln, sb_sp = sem("sb_ps"), sem("sb_abs"), sem("sb_ln"), sem("sb_sp")
        sb_cum, sb_arg, sb_a = sem("sb_cum"), sem("sb_arg"), sem("sb_a")
        o_sq, o_ss, o_r, o_ready = sem("o_sq"), sem("o_ss"), sem("o_r"), sem("o_ready")
        oT_ps, oT_d, oT_a = sem("oT_ps"), sem("oT_d"), sem("oT_a")
        oproj_ps, x_attn = sem("oproj_ps"), sem("x_attn")
        lg_ps, rt_diff, rt_exp, rt_asg = sem("lg_ps"), sem("rt_diff"), sem("rt_exp"), sem("rt_asg")
        pos_ps, routed = sem("pos_ps"), sem("routed")
        STEPS = ["sel_ready", "selw_ready", "gathered", "selwT_ps", "hg_d", "hg_a", "selwT_out", "gu_ps", "gate_exp",
                 "act_out", "actT_ps", "actT_out", "dn0_ps", "dn1_ps", "y_d", "y_a", "sc0_ps", "sc1_ps"]
        first = {n: sem(n) for n in STEPS}
        more = {n: sem("more_" + n) for n in STEPS}
        x_moe, x_more, x_done = sem("x_moe"), sem("x_more"), sem("x_done")
        dn_used = sem("dn_used")
        PE_MORE = [more[n] for n in ("gathered", "selwT_ps", "gu_ps", "actT_ps", "dn0_ps", "dn1_ps", "sc0_ps", "sc1_ps")]
        ACT_MORE = [more[n] for n in ("hg_a", "gate_exp", "y_a")]
        DVE_MORE = [more[n] for n in ("sel_ready", "selw_ready", "hg_d", "selwT_out", "act_out", "actT_out", "y_d")] + [x_more]

        def bcast(v, n):
            return v.unsqueeze(0).broadcast_to([P, n])

        def params(l):
            yield qkg[:, 0, :], bcast(q_norm_g[l], HD)
            yield qkg[:, 1, :], bcast(k_norm_g[l], HD)
            for n, v in enumerate((lambda_q1, lambda_k1, lambda_q2, lambda_k2)):
                yield lamv[:, n, :], bcast(v[l], HD)
            yield dag[:, :], bcast(da_out_g[l], 2 * HD)
            yield sbg[:, :], bcast(sb_out_g[l], HD)
            yield g2[:, :], bcast(norm2_g[l], D)
            yield wr[:, :, 0:GROUPS], w_router_group[l].rearrange("(p k) n -> p k n", k=KC)
            yield wr[:, :, GROUPS:], w_router_expert[l].rearrange("(p k) n -> p k n", k=KC)
            yield br[:, 0:GROUPS], bcast(b_router_group[l], GROUPS)
            yield br[:, GROUPS:], bcast(b_router_expert[l], EXPERTS)
        N_PAR = 13 * 16

        w_gate_e = w_gate.rearrange("l e (p k) f -> (l e) p (k f)", k=KC)
        w_up_e = w_up.rearrange("l e (p k) f -> (l e) p (k f)", k=KC)
        w_down_e = w_down.rearrange("l e (p c) d -> (l e) p (c d)", c=FC)

        MORE = ROUNDS - 1
        GATHERS = SETS + 1

        def second_round_early(eng, n_set, most, early):
            with eng.If(most > SLOTS):
                early(eng.snap(n_set * MORE + 1))

        def further_rounds(eng, n_set, most, late, whole, owed):
            base = eng.snap(n_set * MORE)
            with eng.If(most > SLOTS):
                late(eng.snap(base + 1))
                with eng.If(most > 2 * SLOTS):
                    with eng.Fori(2, ROUNDS) as r:
                        with eng.If(most > r * SLOTS):
                            whole(eng.snap(base + r), r)
                        with eng.Else():
                            eng.drain()
                            for s in owed:
                                eng.sem_inc(s, 1)
                with eng.Else():
                    eng.drain()
                    for s in owed:
                        eng.sem_inc(s, MORE - 1)
            with eng.Else():
                eng.drain()
                for s in owed:
                    eng.sem_inc(s, MORE)

        block = ctx.enter_context(nc.Block())

        @block.sync
        def _(sp_):
            def load_block(l, i):
                free = l * UNITS + (-LANES, -LANES, 0, 0, 0, 0, 1, 2)[i]
                if free > 0:
                    sp_.wait_ge(slot_used, free)
                w, c = (w_in, ORDER[i] * HALF) if i < len(ORDER) else (w_out, (i - len(ORDER)) * HALF)
                dst = wbuf[:, block_slot(l, i), :].rearrange("p (k c) -> p k c", k=KC)
                src = w[l, :, c:c + HALF].rearrange("(k p) c -> p k c", p=P)
                if i == 0:
                    sp_.dma_start(dst[:, 0:KC // 2, :], src[:, 0:KC // 2, :]).then_inc(block_in[0], 16)
                    sp_.dma_start(dst[:, KC // 2:, :], src[:, KC // 2:, :]).then_inc(block0_rest_in, 16)
                else:
                    sp_.dma_start(dst, src).then_inc(block_in[i], 16)

            def load_gu(l, g, parity, j):
                e = g * LANES + (l * EXPERTS + j)
                for h, w in enumerate((w_gate_e, w_up_e)):
                    sp_.dma_start(wbuf[:, lane_slot(l, parity, j), h * KC * FF:(h + 1) * KC * FF], w[e])\
                       .then_inc(gu_in[j], 16)

            def load_set(l, g, parity):
                sp_.wait_ge(slot_used, g * LANES + (l * UNITS + BLOCKS - LANES))
                load_gu(l, g, parity, 0)
                load_gu(l, g, parity, 1)
                sp_.wait_ge(slot_used, g * LANES + (l * UNITS + BLOCKS))
                load_gu(l, g, parity, 2)
                load_gu(l, g, parity, 3)
                sp_.wait_ge(dn_used, g + l * SETS)
                for j in range(LANES):
                    load_dn(l, g, j)

            def load_dn(l, g, j):
                sp_.dma_start(dnbuf[:, j, :], w_down_e[g * LANES + (l * EXPERTS + j)]).then_inc(dn_in[j], 16)

            sp_.dma_start(x_sb[:, 0, :], x[0, 0:P, :]).then_inc(x_in[0], 16)
            sp_.dma_start(g1[:, :], bcast(norm1_g[0], D)).then_inc(g1_in[0], 16)
            sp_.dma_start(ident, const[:, C_ID:C_GE]).then_inc(ident_in, 16)
            sp_.dma_start(x_sb[:, 1, :], x[0, P:2 * P, :]).then_inc(x_in[1], 16)
            for l in range(DEPTH):
                for i in range(BLOCKS):
                    load_block(l, i)
                    if l == 0 and i == 0:
                        sp_.dma_start(cst[:, C_GE:], const[:, C_GE:]).then_inc(const_in, 16)
                        for dst, src in params(0):
                            sp_.dma_start(dst, src).then_inc(par_in[0], 16)
                for j in range(LANES):
                    sp_.wait_ge(slot_used, l * UNITS + 3 + j)
                    load_gu(l, 0, 0, j)
                sp_.wait_ge(o_ready, (l + 1) * TT)
                for j in range(LANES):
                    load_dn(l, 0, j)
                load_set(l, 1, 1)
                with sp_.Fori(1, SETS // 2) as h:
                    load_set(l, sp_.snap(h * 2), 0)
                    load_set(l, sp_.snap(h * 2 + 1), 1)
            sp_.wait_ge(x_done, DEPTH)
            sp_.dma_start(out[0].rearrange("(t p) d -> p t d", p=P), x_sb[:, :, :]).then_inc(out_done, 16)
            sp_.wait_ge(out_done, 16)

        @block.gpsimd
        def _(pool):
            for l in range(1, DEPTH):
                pool.wait_ge(routed, l)
                nc.gpsimd.dma_start(g1[:, :], bcast(norm1_g[l], D)).then_inc(g1_in[l], 16)
                for dst, src in params(l):
                    nc.gpsimd.dma_start(dst, src).then_inc(par_in[l], 16)

        @block.scalar
        def _(act):
            act.preload_act_table_set("natural_log_exp_and_others")

            def scales(out_ap, in_ap, width):
                nc.scalar.activation(out_ap, in_ap, ACT.Ln, bias=EPS, scale=1.0 / width)
                act.drain()
                return nc.scalar.activation(out_ap, out_ap, ACT.Exp, scale=-0.5)

            def norm(l, t):
                nc.scalar.activation(y, x_sb[:, t, :], ACT.Square, accum_out=ssq[:, t:t + 1])
                act.drain()
                scales(rstd[:, t:t + 1], ssq[:, t:t + 1], D).then_inc(norm_r, 1)

            def hT_half(n, t):
                act.wait_ge(hT_ps, n * 2 * TT + 2 * t + 2)
                nc.scalar.copy(hT[:, 4:8, t * P:(t + 1) * P],
                               ps[2 * t + 1][:, :].rearrange("p (k c) -> p k c", k=4)).then_inc(hT_a, 1)

            def proj_tile(l, i, t):
                act.wait_ge(proj_ps, l * 12 + 2 * i + t + 1)
                if i in (2, 3):
                    act.wait_ge(qkT_ps, l * 8 + 2 * (i - 2) + 2)
                dst = stage[:, i % 2, t, :] if i < 4 else v_sb[:, t, i - 4, :]
                nc.scalar.activation(dst, ps[PROJ_BANK[i][t]][:, :], ACT.Copy, scale=rstd[:, t:t + 1]).then_inc(proj_out, 1)

            def proj(l, i):
                for t in range(TT):
                    proj_tile(l, i, t)

            def qk_scale(l, i):
                act.wait_ge(qk_ss, l * 2 + i + 1)
                scales(hr[:, i * 16:i * 16 + 16], hss[:, i * 16:i * 16 + 16], HD).then_inc(qk_r, 1)

            def qkT_half(l, i):
                act.wait_ge(qkT_ps, l * 8 + 2 * i + 2)
                nc.scalar.copy(qk[:, i, :, P:2 * P], ps[QKT_BANK[i][1]][:, :].rearrange("p (a c) -> p a c", a=PAIRS))\
                  .then_inc(qkT_a, 1)

            def softmax_exp(l, u):
                act.wait_ge(da_max, l * 3 + u + 1)
                keys = P if u == 0 else 2 * P
                heads = HALF // keys
                for e in range(2):
                    for h in range(heads):
                        c = e * heads + h
                        s = s_da[:, u, e, h * keys:(h + 1) * keys]
                        last = nc.scalar.activation(s, s, ACT.Exp, bias=dmax[:, u, c:c + 1],
                                                    accum_out=dsum[:, u, c:c + 1])
                act.drain().then_inc(da_exp, 1)

            def softplus_ln(l, ws):
                for w in ws:
                    n = SB_ORDER.index(w)
                    act.wait_ge(sb_abs, l * 6 + n + 1)
                    nc.scalar.activation(sp[w], sp[w], ACT.Exp)
                act.drain()
                for w in ws:
                    nc.scalar.activation(sp[w], sp[w], ACT.Ln, bias=1.0).then_inc(sb_ln, 1)

            def daT_copy(l, u):
                act.wait_ge(daT_ps, l * 3 + u + 1)
                nc.scalar.copy(aT[u], ps[DAT_BANK[u]][:, :].rearrange("p (b c) -> p b c", b=4)).then_inc(daT_out, 1)

            def break_exp(l, w):
                act.wait_ge(sb_arg, l * 6 + SB_ORDER.index(w) + 1)
                nc.scalar.activation(zm[:, w, :], zm[:, w, :], ACT.Exp).then_inc(sb_a, 1)

            def gather_copy(s, n, dst):
                act.wait_ge(s["gathered"], n)
                nc.scalar.copy(dst[:, 4:8, :], ps[1][:, :].rearrange("p (k s) -> p k s", k=4)).then_inc(s["hg_a"], 1)

            def gate(s, n):
                act.wait_ge(s["gu_ps"], n)
                nc.scalar.activation(eg, ps[2][:, 0:FF], ACT.Exp, scale=-1.0).then_inc(s["gate_exp"], 1)

            def y_copy(s, n):
                act.wait_ge(s["dn1_ps"], n)
                nc.scalar.copy(y[:, HALF:], ps[5][:, :]).then_inc(s["y_a"], 1)

            def early(n):
                gather_copy(more, n, hgT_more)
                gate(more, n)

            def late(n):
                y_copy(more, n)

            def whole(n, r):
                early(n)
                late(n)

            for l in range(DEPTH):
                if l == 0:
                    act.wait_ge(x_in[0], 16)
                else:
                    act.wait_ge(x_done, l)
                norm(l, 0)
                hT_half(2 * l, 0)
                if l == 0:
                    act.wait_ge(x_in[1], 16)
                norm(l, 1)
                hT_half(2 * l, 1)
                act.wait_ge(lam_dot, l + 1)
                nc.scalar.activation(lams[:, 2:4], lams[:, 0:2], ACT.Exp).then_inc(lam_exp, 1)
                proj(l, 0)
                qk_scale(l, 0)
                proj(l, 1)
                qk_scale(l, 1)
                qkT_half(l, 0)
                proj(l, 2)
                qkT_half(l, 1)
                softmax_exp(l, 0)
                softmax_exp(l, 1)
                proj(l, 3)
                softmax_exp(l, 2)
                qkT_half(l, 2)
                daT_copy(l, 0)
                daT_copy(l, 1)
                qkT_half(l, 3)
                softplus_ln(l, (4, 5))
                daT_copy(l, 2)
                softplus_ln(l, (0, 1))
                proj_tile(l, 4, 0)
                softplus_ln(l, (2, 3))
                proj_tile(l, 4, 1)
                break_exp(l, 4)
                break_exp(l, 5)
                proj_tile(l, 5, 0)
                break_exp(l, 0)
                break_exp(l, 1)
                proj_tile(l, 5, 1)
                break_exp(l, 2)
                break_exp(l, 3)
                for t in range(TT):
                    act.wait_ge(o_ps, l * TT + t + 1)
                    nc.scalar.activation(osq[:, 2 * t, :], ps[DAO_BANK[t]][:, :], ACT.Square)
                    nc.scalar.activation(osq[:, 2 * t + 1, :], ps[SBO_BANK[t]][:, :], ACT.Square)
                    act.drain().then_inc(o_sq, 1)
                    act.wait_ge(o_ss, l * TT + t + 1)
                    scales(oss[:, t, 12:16], oss[:, t, 0:4], 2 * HD)
                    scales(oss[:, t, 16:24], oss[:, t, 4:12], HD)
                    act.drain().then_inc(o_r, 1)
                for t in range(TT):
                    act.wait_ge(oT_ps, l * 4 + 2 * t + 2)
                    nc.scalar.copy(hT[:, 4:8, t * P:(t + 1) * P],
                                   ps[OT_BANK[t][1]][:, :].rearrange("p (k c) -> p k c", k=4)).then_inc(oT_a, 1)
                for t in range(TT):
                    act.wait_ge(x_attn, l * 2 * TT + 2 * (t + 1))
                    norm(l, t)
                    hT_half(2 * l + 1, t)
                act.wait_ge(rt_diff, 2 * l + 1)
                nc.scalar.activation(r4[:, 1], r4[:, 0], ACT.Exp).then_inc(rt_exp, 1)
                act.wait_ge(rt_diff, 2 * l + 2)
                nc.scalar.activation(rs[:, 5, :], rs[:, 4, :], ACT.Exp).then_inc(rt_exp, 1)
                act.wait_ge(routed, l + 1)
                gather_copy(first, l * GATHERS + 1, hgT)
                with act.Fori(0, SETS) as g:
                    most = act.value_load(cnt[0:1, bass.ds(g, 1)], min_val=0, max_val=SEQ)
                    gate(first, act.snap(g + l * SETS + 1))
                    gather_copy(first, act.snap(g + l * GATHERS + 2), hgT)
                    second_round_early(act, g + l * SETS, most, early)
                    y_copy(first, act.snap(g + l * SETS + 1))
                    further_rounds(act, g + l * SETS, most, late, whole, ACT_MORE)

        @block.vector
        def _(dve):
            V = nc.vector
            gap = dve.drain

            def hT_half(n, t):
                dve.wait_ge(hT_ps, n * 2 * TT + 2 * t + 1)
                V.tensor_copy(hT[:, 0:4, t * P:(t + 1) * P],
                              ps[2 * t][:, :].rearrange("p (k c) -> p k c", k=4)).then_inc(hT_d, 1)

            def qk_norm(l, i):
                b = stage[:, i, :, :]
                rows = b.rearrange("p t c -> p (t c)")
                heads = rows.rearrange("p (h c) -> p h c", c=HD)
                dve.wait_ge(proj_out, l * 12 + 2 * i + 2)
                V.tensor_tensor(sq, rows, rows, ALU.mult)
                gap()
                V.tensor_reduce(hss[:, i * 16:i * 16 + 16], sq.rearrange("p (h c) -> p h c", c=HD),
                                AX.X, ALU.add).then_inc(qk_ss, 1)
                dve.wait_ge(qk_r, l * 2 + i + 1)
                V.tensor_tensor(heads, heads, hr[:, i * 16:i * 16 + 16].unsqueeze(2).broadcast_to([P, 16, HD]), ALU.mult)
                gap()
                V.tensor_tensor(heads, heads, over(qkg[:, i, :], 16), ALU.mult)
                gap()
                for t in range(TT):
                    h = b[:, t, :].rearrange("p (h c) -> p h c", c=HD)
                    first, second = h[:, :, 0:ROPE], h[:, :, ROPE:2 * ROPE]
                    cos = over(cst[:, C_COS + t * ROPE:C_COS + (t + 1) * ROPE], 8)
                    sin = over(cst[:, C_SIN + t * ROPE:C_SIN + (t + 1) * ROPE], 8)
                    part = [rope[:, n, t * 8 * ROPE:(t + 1) * 8 * ROPE].rearrange("p (h c) -> p h c", c=ROPE) for n in range(4)]
                    V.tensor_tensor(part[0], first, cos, ALU.mult)
                    V.tensor_tensor(part[1], second, sin, ALU.mult)
                    V.tensor_tensor(part[2], second, cos, ALU.mult)
                    V.tensor_tensor(part[3], first, sin, ALU.mult)
                gap()
                for t in range(TT):
                    h = b[:, t, :].rearrange("p (h c) -> p h c", c=HD)
                    part = [rope[:, n, t * 8 * ROPE:(t + 1) * 8 * ROPE].rearrange("p (h c) -> p h c", c=ROPE) for n in range(4)]
                    V.tensor_tensor(h[:, :, 0:ROPE], part[0], part[1], ALU.subtract)
                    last = V.tensor_tensor(h[:, :, ROPE:2 * ROPE], part[2], part[3], ALU.add)
                gap().then_inc(qk_normed, 1)

            def qkT_half(l, i):
                dve.wait_ge(qkT_ps, l * 8 + 2 * i + 1)
                V.tensor_copy(qk[:, i, :, 0:P], ps[QKT_BANK[i][0]][:, :].rearrange("p (a c) -> p a c", a=PAIRS))\
                 .then_inc(qkT_d, 1)

            def da_scores(l, u):
                keys = P if u == 0 else 2 * P
                heads = HALF // keys
                mask = cst[:, C_MQ + (P if u == 0 else 0):C_MQ + 2 * P]
                dve.wait_ge(da_ps, l * 3 + u + 1)
                for e in range(2):
                    V.scalar_tensor_tensor(s_da[:, u, e, :].rearrange("p (h c) -> p h c", h=heads),
                                           ps[DAS_BANK[u][e]][:, :].rearrange("p (h c) -> p h c", h=heads),
                                           SCALE, over(mask, heads), ALU.mult, ALU.add)
                gap()
                V.tensor_reduce(dmax[:, u, 0:2 * heads], s_da[:, u].rearrange("p e (h c) -> p (e h) c", h=heads),
                                AX.X, ALU.max, negate=True).then_inc(da_max, 1)

            def da_mix_(l, u):
                keys = P if u == 0 else 2 * P
                heads = HALF // keys
                dve.wait_ge(da_exp, l * 3 + u + 1)
                V.reciprocal(dsum[:, u, 0:2 * heads], dsum[:, u, 0:2 * heads])
                gap()
                V.tensor_scalar(dsum[:, u, heads:2 * heads], dsum[:, u, heads:2 * heads], lams[:, 0:1], None, ALU.mult)
                gap()
                for h in range(heads):
                    c = slice(h * keys, (h + 1) * keys)
                    V.tensor_scalar(s_da[:, u, 0, c], s_da[:, u, 0, c], dsum[:, u, h:h + 1], None, ALU.mult)
                gap()
                for h in range(heads):
                    c = slice(h * keys, (h + 1) * keys)
                    V.scalar_tensor_tensor(s_da[:, u, 0, c], s_da[:, u, 1, c], dsum[:, u, heads + h:heads + h + 1],
                                           s_da[:, u, 0, c], ALU.mult, ALU.add)
                gap().then_inc(da_mix, 1)

            def sb_scores(l, ws):
                for w in ws:
                    heads = 4 if w >= 4 else 2
                    mask = cst[:, C_MS:C_MS + (P if w >= 4 else 2 * P)]
                    dve.wait_ge(sb_ps, l * 6 + SB_ORDER.index(w) + 1)
                    V.scalar_tensor_tensor(zm[:, w, :].rearrange("p (h c) -> p h c", h=heads),
                                           ps[SB_BANK[w]][:, :].rearrange("p (h c) -> p h c", h=heads),
                                           SCALE, over(mask, heads), ALU.mult, ALU.add)
                gap()
                for w in ws:
                    V.scalar_tensor_tensor(sp[w], zm[:, w, :], -1.0, zm[:, w, :], ALU.mult, ALU.min).then_inc(sb_abs, 1)

            def sb_softplus(l, ws):
                for w in ws:
                    dve.wait_ge(sb_ln, l * 6 + SB_ORDER.index(w) + 1)
                    V.scalar_tensor_tensor(sp[w], zm[:, w, :], 0.0, sp[w], ALU.max, ALU.add).then_inc(sb_sp, 1)

            def sb_argument(l, w):
                dve.wait_ge(sb_cum, l * 6 + SB_ORDER.index(w) + 1)
                V.tensor_tensor(zm[:, w, :], zm[:, w, :], ps[SB_BANK[w]][:, :], ALU.subtract).then_inc(sb_arg, 1)

            def first_of(onehot, values, top, weights):
                V.tensor_tensor(onehot, values, top.unsqueeze(2).broadcast_to(list(values.shape)), ALU.is_equal)
                gap()
                V.tensor_tensor(onehot, onehot, over(weights, TT), ALU.mult)
                gap()
                V.tensor_reduce(rs[:, 7, :], onehot, AX.X, ALU.max)
                gap()
                V.tensor_tensor(onehot, onehot, rs[:, 7, :].unsqueeze(2).broadcast_to(list(values.shape)), ALU.is_equal)
                gap()

            def select(s, g, r):
                shape = [P, LANES, SLOTS]
                slot = cst[:, C_IOTA:C_REV].rearrange("p (j s) -> p j s", j=LANES)
                rank = [pos[:, t, 0:LANES] if g is None else posg[:, t, :] for t in range(TT)]
                weight = [wgt[:, t, 0:LANES] if g is None else wgg[:, t, :] for t in range(TT)]
                if g is not None:
                    for t in range(TT):
                        V.tensor_copy(posg[:, t, :], pos[:, t, bass.ds(g * LANES, LANES)])
                        V.tensor_copy(wgg[:, t, :], wgt[:, t, bass.ds(g * LANES, LANES)])
                    gap()
                if r is not None:
                    V.tensor_tensor(posg[:, :, :], posg[:, :, :],
                                    cst[:, bass.ds(r + C_OFF, 1)].unsqueeze(2).broadcast_to([P, TT, LANES]), ALU.subtract)
                    gap()
                for t in range(TT):
                    V.tensor_tensor(sel[:, t, :].rearrange("p (j s) -> p j s", j=LANES), slot,
                                    rank[t].unsqueeze(2).broadcast_to(shape), ALU.is_equal)
                gap().then_inc(s["sel_ready"], 1)
                for t in range(TT):
                    V.tensor_tensor(selw[:, t, :].rearrange("p (j s) -> p j s", j=LANES),
                                    sel[:, t, :].rearrange("p (j s) -> p j s", j=LANES),
                                    weight[t].unsqueeze(2).broadcast_to(shape), ALU.mult)
                gap().then_inc(s["selw_ready"], 1)

            def gather_copy(s, n, dst, dst_w, bank):
                dve.wait_ge(s["gathered"], n)
                V.tensor_copy(dst[:, 0:4, :], ps[0][:, :].rearrange("p (k s) -> p k s", k=4)).then_inc(s["hg_d"], 1)
                dve.wait_ge(s["selwT_ps"], n)
                V.tensor_copy(dst_w.rearrange("p t s -> p (t s)"), ps[bank][:, 0:TT * P]).then_inc(s["selwT_out"], 1)

            def activate(s, n):
                dve.wait_ge(s["gate_exp"], n)
                V.tensor_scalar(rg, eg, 1.0, None, ALU.add)
                gap()
                V.reciprocal(rg, rg)
                gap()
                V.tensor_tensor(tg, ps[2][:, 0:FF], rg, ALU.mult)
                gap()
                V.tensor_tensor(act_sb.rearrange("p (c f) -> p f c", c=FC),
                                ps[2][:, FF:2 * FF].rearrange("p (f c) -> p f c", c=FC),
                                tg.rearrange("p (f c) -> p f c", c=FC), ALU.mult).then_inc(s["act_out"], 1)

            def act_copy(s, n):
                dve.wait_ge(s["actT_ps"], n)
                V.tensor_copy(actT.rearrange("p c s -> p (c s)"), ps[3][:, 0:FF]).then_inc(s["actT_out"], 1)

            def into_x(s, n, done):
                dve.wait_ge(s["dn0_ps"], n)
                V.tensor_copy(y[:, 0:HALF], ps[4][:, :]).then_inc(s["y_d"], 1)
                for t in range(TT):
                    dve.wait_ge(s[f"sc{t}_ps"], n)
                    for h in range(2):
                        c = slice(h * HALF, (h + 1) * HALF)
                        V.tensor_tensor(x_sb[:, t, c], x_sb[:, t, c], ps[SC_BANK[t][h]][:, :], ALU.add)
                gap().then_inc(done, 1)

            def expert_set(l, g, parity):
                most = dve.value_load(cnt[0:1, bass.ds(g, 1)], min_val=0, max_val=SEQ)
                dve.wait_ge(first["selwT_ps"], g + (l * GATHERS + 1))
                select(first, g + 1, None)
                n = dve.snap(g + l * SETS + 1)
                activate(first, n)
                act_copy(first, n)
                gather_copy(first, dve.snap(g + l * GATHERS + 2), hgT, selwT2[1 - parity], 6)

                def early(m, r=1):
                    select(more, g, r)
                    gather_copy(more, m, hgT_more, selwT_more, 7)
                    activate(more, m)

                def late(m):
                    act_copy(more, m)
                    into_x(more, m, x_more)

                def whole(m, r):
                    early(m, r)
                    late(m)
                second_round_early(dve, g + l * SETS, most, early)
                into_x(first, n, x_moe)
                further_rounds(dve, g + l * SETS, most, late, whole, DVE_MORE)

            dve.sem_inc(x_moe, 1)
            dve.sem_inc(x_more, 1)
            V.memset(pos[:, :, EXPERTS:], -1.0)
            V.memset(wgt[:, :, EXPERTS:], 0.0)
            for l in range(DEPTH):
                lam_init = 0.8 - 0.6 * math.exp(-0.3 * l)
                dve.wait_ge(g1_in[l], 16)
                for t in range(TT):
                    if l == 0:
                        dve.wait_ge(x_in[t], 16)
                    V.tensor_tensor(xn[:, t, :], x_sb[:, t, :], g1[:, :], ALU.mult).then_inc(h_ready, 1)
                for t in range(TT):
                    hT_half(2 * l, t)
                if l == 0:
                    dve.wait_ge(const_in, 16)
                dve.wait_ge(par_in[l], N_PAR)
                prod = sq[:, 0:2 * HD].rearrange("p (n c) -> p n c", n=2)
                V.tensor_tensor(prod, lamv[:, 0:4:2, :], lamv[:, 1:4:2, :], ALU.mult)
                gap()
                V.tensor_reduce(lams[:, 0:2], prod, AX.X, ALU.add).then_inc(lam_dot, 1)
                dve.wait_ge(lam_exp, l + 1)
                V.tensor_scalar(lams[:, 0:1], lams[:, 3:4], lams[:, 2:3], -lam_init, ALU.subtract, ALU.add)
                gap()
                qk_norm(l, 0)
                qk_norm(l, 1)
                qkT_half(l, 0)
                qkT_half(l, 1)
                da_scores(l, 0)
                da_scores(l, 1)
                da_mix_(l, 0)
                da_mix_(l, 1)
                da_scores(l, 2)
                qkT_half(l, 2)
                qkT_half(l, 3)
                da_mix_(l, 2)
                sb_scores(l, (4, 5))
                sb_scores(l, (0, 1))
                sb_softplus(l, (4, 5))
                sb_scores(l, (2, 3))
                sb_softplus(l, (0, 1))
                sb_softplus(l, (2, 3))
                for w in SB_ORDER:
                    sb_argument(l, w)
                for t in range(TT):
                    dve.wait_ge(o_sq, l * TT + t + 1)
                    V.tensor_reduce(oss[:, t, 0:4], osq[:, 2 * t, :].rearrange("p (h c) -> p h c", c=2 * HD), AX.X, ALU.add)
                    V.tensor_reduce(oss[:, t, 4:12], osq[:, 2 * t + 1, :].rearrange("p (h c) -> p h c", c=HD), AX.X, ALU.add)
                    gap().then_inc(o_ss, 1)
                    dve.wait_ge(o_r, l * TT + t + 1)
                    o_da = xn[:, t, 0:HALF].rearrange("p (h c) -> p h c", c=2 * HD)
                    o_sb = xn[:, t, HALF:].rearrange("p (h c) -> p h c", c=HD)
                    V.tensor_tensor(o_da, ps[DAO_BANK[t]][:, :].rearrange("p (h c) -> p h c", c=2 * HD),
                                    oss[:, t, 12:16].unsqueeze(2).broadcast_to([P, 4, 2 * HD]), ALU.mult)
                    V.tensor_tensor(o_sb, ps[SBO_BANK[t]][:, :].rearrange("p (h c) -> p h c", c=HD),
                                    oss[:, t, 16:24].unsqueeze(2).broadcast_to([P, 8, HD]), ALU.mult)
                    gap()
                    V.scalar_tensor_tensor(o_da, o_da, 1.0 - lam_init, over(dag[:, :], 4), ALU.mult, ALU.mult)
                    V.tensor_tensor(o_sb, o_sb, over(sbg[:, :], 8), ALU.mult)
                    gap().then_inc(o_ready, 1)
                for t in range(TT):
                    dve.wait_ge(oT_ps, l * 4 + 2 * t + 1)
                    V.tensor_copy(hT[:, 0:4, t * P:(t + 1) * P],
                                  ps[OT_BANK[t][0]][:, :].rearrange("p (k c) -> p k c", k=4)).then_inc(oT_d, 1)
                for t in range(TT):
                    for h in range(2):
                        dve.wait_ge(oproj_ps, l * 4 + 2 * t + h + 1)
                        c = slice(h * HALF, (h + 1) * HALF)
                        V.tensor_tensor(x_sb[:, t, c], x_sb[:, t, c], ps[OP_BANK[t][h]][:, :], ALU.add).then_inc(x_attn, 1)
                        if t == 1 and h == 0:
                            hT_half(2 * l + 1, 0)
                    gap()
                    V.tensor_tensor(xn[:, t, :].rearrange("p (k c) -> p c k", k=KC),
                                    x_sb[:, t, :].rearrange("p (c k) -> p c k", k=KC),
                                    g2[:, :].rearrange("p (c k) -> p c k", k=KC), ALU.mult).then_inc(h_ready, 1)
                hT_half(2 * l + 1, 1)
                dve.wait_ge(hT_ps, (2 * l + 2) * 2 * TT)
                for t in range(TT):
                    dve.wait_ge(norm_r, 4 * l + 2 + t + 1)
                    V.tensor_scalar(xn[:, t, :], xn[:, t, :], rstd[:, t:t + 1], None, ALU.mult)
                dve.wait_ge(lg_ps, l + 1)
                for t in range(TT):
                    V.scalar_tensor_tensor(lg[:, t, :], ps[4][:, t * 64:t * 64 + GROUPS + EXPERTS], rstd[:, t:t + 1],
                                           br[:, :], ALU.mult, ALU.add)
                gap()
                gl, el = lg[:, :, 0:GROUPS], lg[:, :, GROUPS:]
                V.tensor_reduce(rs[:, 0, :], gl, AX.X, ALU.max)
                gap()
                V.tensor_tensor(r4[:, 0], gl, rs[:, 0, :].unsqueeze(2).broadcast_to([P, TT, GROUPS]), ALU.subtract).then_inc(rt_diff, 1)
                first_of(r4[:, 2], gl, rs[:, 0, :], cst[:, C_REV:C_REV + GROUPS])
                V.tensor_scalar(r4[:, 3], r4[:, 2], -NEG, NEG, ALU.mult, ALU.add)
                gap()
                for t in range(TT):
                    V.tensor_tensor(em[:, t, :].rearrange("p (g e) -> p g e", g=GROUPS),
                                    el[:, t, :].rearrange("p (g e) -> p g e", g=GROUPS),
                                    r4[:, 3, t, :].unsqueeze(2).broadcast_to([P, GROUPS, PER_GROUP]), ALU.add)
                gap()
                V.tensor_reduce(rs[:, 1, :], em[:, :, :], AX.X, ALU.max)
                gap()
                first_of(oh1[:, :, :], em[:, :, :], rs[:, 1, :], cst[:, C_REV:C_OFF])
                V.scalar_tensor_tensor(ev[:, :, :], oh1[:, :, :], 3 * NEG, em[:, :, :], ALU.mult, ALU.add)
                gap()
                V.tensor_reduce(rs[:, 2, :], ev[:, :, :], AX.X, ALU.max)
                gap()
                V.tensor_tensor(rs[:, 4, :], rs[:, 2, :], rs[:, 1, :], ALU.subtract).then_inc(rt_diff, 1)
                first_of(oh2[:, :, :], ev[:, :, :], rs[:, 2, :], cst[:, C_REV:C_OFF])
                V.tensor_tensor(asg[:, 0:TT, :], oh1[:, :, :], oh2[:, :, :], ALU.add)
                gap().then_inc(rt_asg, 1)
                V.tensor_tensor(asg[:, TT, :], asg[:, 0, :], asg[:, 1, :], ALU.add).then_inc(rt_asg, 1)
                dve.wait_ge(rt_exp, 2 * l + 2)
                V.tensor_reduce(rs[:, 3, :], r4[:, 1], AX.X, ALU.add)
                V.tensor_scalar(rs[:, 6, :], rs[:, 5, :], 1.0, None, ALU.add)
                gap()
                V.tensor_tensor(rs[:, 3, :], rs[:, 3, :], rs[:, 6, :], ALU.mult)
                gap()
                V.reciprocal(rs[:, 3, :], rs[:, 3, :])
                gap()
                V.tensor_tensor(rs[:, 6, :], rs[:, 3, :], rs[:, 5, :], ALU.mult)
                gap()
                for t in range(TT):
                    V.tensor_scalar(wgt[:, t, 0:EXPERTS], oh1[:, t, :], rs[:, 3, t:t + 1], None, ALU.mult)
                gap()
                for t in range(TT):
                    V.scalar_tensor_tensor(wgt[:, t, 0:EXPERTS], oh2[:, t, :], rs[:, 6, t:t + 1], wgt[:, t, 0:EXPERTS], ALU.mult, ALU.add)
                dve.wait_ge(pos_ps, l + 1)
                V.scalar_tensor_tensor(pos[:, :, 0:EXPERTS], ps[5][:, 0:2 * EXPERTS].rearrange("p (t e) -> p t e", t=TT), 1.0,
                                       asg[:, 0:TT, :], ALU.add, ALU.mult)
                V.tensor_reduce(cntf[:, :], ps[5][:, 2 * EXPERTS:3 * EXPERTS].rearrange("p (g j) -> p g j", j=LANES), AX.X, ALU.max)
                gap()
                V.tensor_scalar(pos[:, :, 0:EXPERTS], pos[:, :, 0:EXPERTS], -1.0, None, ALU.add)
                V.tensor_copy(cnt[:, :], cntf[:, :])
                gap().then_inc(routed, 1)
                select(first, None, None)
                gather_copy(first, l * GATHERS + 1, hgT, selwT2[0], 6)
                with dve.Fori(0, SETS // 2) as pair:
                    for parity in range(2):
                        expert_set(l, dve.snap(pair * 2 + parity), parity)
                gap().then_inc(x_done, 1)

        @block.tensor
        def _(pe):
            MM, TR = nc.tensor.matmul, nc.tensor.transpose

            def transpose_x(n, t):
                pe.wait_ge(h_ready, n * TT + t + 1)
                for k in range(KC):
                    last = TR(ps[2 * t + k // 4][:, (k % 4) * P:(k % 4 + 1) * P], xn[:, t, k * P:(k + 1) * P], ident)
                    if k % 4 == 3:
                        last.then_inc(hT_ps, 1)

            def block_of(l, i):
                return wbuf[:, block_slot(l, i), :].rearrange("p (k c) -> p k c", k=KC)

            def proj_tile(l, i, t):
                if t == 0:
                    pe.wait_ge(block_in[i], (l + 1) * 16)
                if i == 0:
                    pe.wait_ge(hT_d, 2 * l * TT + t + 1)
                    pe.wait_ge(hT_a, 2 * l * TT + t + 1)
                if i >= 2:
                    before = i - 1 if i == 5 else i - 2
                    pe.wait_ge(proj_out, l * 12 + 2 * before + t + 1)
                w = block_of(l, i)
                for k in range(KC):
                    if i == 0 and k == KC // 2:
                        pe.wait_ge(block0_rest_in, (l + 1) * 16)
                    last = MM(ps[PROJ_BANK[i][t]][:, :], hT[:, k, t * P:(t + 1) * P], w[:, k, :],
                              start=(k == 0), stop=(k == KC - 1))
                last.then_inc(proj_ps, 1)
                if t == TT - 1:
                    pe.drain().then_inc(slot_used, 1)

            def proj(l, i):
                for t in range(TT):
                    proj_tile(l, i, t)

            def transpose_qk(l, i):
                if i < 2:
                    pe.wait_ge(qk_normed, l * 2 + i + 1)
                else:
                    pe.wait_ge(proj_out, l * 12 + 2 * i + 2)
                if i == 0:
                    pe.wait_ge(hT_a, 2 * l * TT + TT)
                    pe.wait_ge(hT_d, 2 * l * TT + TT)
                if i >= 2:
                    pe.wait_ge(da_max, l * 3 + i)
                for t in range(TT):
                    for a in range(PAIRS):
                        last = TR(ps[QKT_BANK[i][t]][:, a * P:(a + 1) * P], stage[:, i % 2, t, a * P:(a + 1) * P], ident)
                    last.then_inc(qkT_ps, 1)

            def da_scores(l, u):
                keys = P if u == 0 else 2 * P
                heads = HALF // keys
                q0 = 0 if u == 0 else P
                a0 = 2 if u == 2 else 0
                for h in range(heads):
                    for e in range(2):
                        rows = slice(e * HD, (e + 1) * HD)
                        last = MM(ps[DAS_BANK[u][e]][:, h * keys:(h + 1) * keys], qk[rows, 0, a0 + h, q0:q0 + P],
                                  qk[rows, 1, a0 + h, 0:keys], start=True, stop=True)
                pe.drain().then_inc(da_ps, 1)

            def sb_scores(l, we, wo):
                kt = 1 if we >= 4 else 0
                heads = 4 if kt else 2
                a0 = we if not kt else 0
                for h in range(heads):
                    for e, w in enumerate((we, wo)):
                        rows = slice(e * HD, (e + 1) * HD)
                        n = SEQ - kt * P
                        MM(ps[SB_BANK[w]][:, h * n:(h + 1) * n], qk[rows, 3, a0 + h, kt * P:(kt + 1) * P],
                           qk[rows, 2, a0 + h, kt * P:SEQ], start=True, stop=True)
                pe.drain().then_inc(sb_ps, 2)

            def da_transpose(l, u):
                pe.wait_ge(da_mix, l * 3 + u + 1)
                for b in range(4):
                    last = TR(ps[DAT_BANK[u]][:, b * P:(b + 1) * P], s_da[:, u, 0, b * P:(b + 1) * P], ident)
                last.then_inc(daT_ps, 1)

            def cumulate(l, w):
                pe.wait_ge(sb_sp, l * 6 + SB_ORDER.index(w) + 1)
                MM(ps[SB_BANK[w]][:, :], tri_ge, sp[w], start=True, stop=(w >= 4))
                if w < 4:
                    MM(ps[SB_BANK[w]][:, :].rearrange("p (h q) -> p h q", h=2)[:, :, P:], ones,
                       sp[4 + w % 2][:, (w // 2) * 2 * P:(w // 2 + 1) * 2 * P].rearrange("p (h q) -> p h q", h=2),
                       start=False, stop=True)
                pe.drain().then_inc(sb_cum, 1)

            def router(l, t):
                pe.wait_ge(hT_d, (2 * l + 1) * TT + t + 1)
                pe.wait_ge(hT_a, (2 * l + 1) * TT + t + 1)
                for k in range(KC):
                    last = MM(ps[4][:, t * 64:t * 64 + GROUPS + EXPERTS], hT[:, k, t * P:(t + 1) * P], wr[:, k, :],
                              start=(k == 0), stop=(k == KC - 1))
                if t == TT - 1:
                    last.then_inc(lg_ps, 1)

            def ranks(l):
                pe.wait_ge(rt_asg, 2 * l + 1)
                MM(ps[5][:, 0:TT * EXPERTS], tri_lt, asg[:, 0:TT, :], start=True, stop=False)
                MM(ps[5][:, EXPERTS:2 * EXPERTS], ones, asg[:, 0, :], start=False, stop=True)
                pe.wait_ge(rt_asg, 2 * l + 2)
                MM(ps[5][:, 2 * EXPERTS:3 * EXPERTS], ones, asg[:, TT, :], start=True, stop=True).then_inc(pos_ps, 1)

            def gather(s, n):
                pe.wait_ge(s["sel_ready"], n)
                for k in range(KC):
                    for t in range(TT):
                        last = MM(ps[k // 4][:, (k % 4) * P:(k % 4 + 1) * P], xn[:, t, k * P:(k + 1) * P], sel[:, t, :],
                                  start=(t == 0), stop=(t == TT - 1))
                last.then_inc(s["gathered"], 1)

            def transpose_weights(s, n, bank):
                pe.wait_ge(s["selw_ready"], n)
                for t in range(TT):
                    last = TR(ps[bank][:, t * P:(t + 1) * P], selw[:, t, :], ident)
                last.then_inc(s["selwT_ps"], 1)

            def gate_up(s, n, src, slots):
                pe.wait_ge(s["hg_d"], n)
                pe.wait_ge(s["hg_a"], n)
                for k in range(KC):
                    for j in range(LANES):
                        w = wbuf[:, slots[j], :].rearrange("p (a k f) -> p a k f", a=2, k=KC)
                        MM(ps[2][j * SLOTS:(j + 1) * SLOTS, :].rearrange("p (a f) -> p a f", a=2),
                           src[:, k, j * SLOTS:(j + 1) * SLOTS], w[:, :, k, :], start=(k == 0), stop=(k == KC - 1))
                pe.drain().then_inc(s["gu_ps"], 1)

            def transpose_act(s, n):
                pe.wait_ge(s["act_out"], n)
                for c in range(FC):
                    last = TR(ps[3][:, c * P:(c + 1) * P], act_sb[:, c * P:(c + 1) * P], ident)
                last.then_inc(s["actT_ps"], 1)
                pe.wait_ge(s["actT_out"], n)

            def down(s):
                for h in range(2):
                    for c in range(FC):
                        for j in range(LANES):
                            MM(ps[4 + h][j * SLOTS:(j + 1) * SLOTS, :], actT[:, c, j * SLOTS:(j + 1) * SLOTS],
                               dnbuf[:, j, c * D + h * HALF:c * D + (h + 1) * HALF], start=(c == 0), stop=(c == FC - 1))
                    pe.drain().then_inc(s[f"dn{h}_ps"], 1)

            def scatter(s, n, weights):
                pe.wait_ge(s["y_d"], n)
                pe.wait_ge(s["y_a"], n)
                for t in range(TT):
                    for h in range(2):
                        last = MM(ps[SC_BANK[t][h]][:, :], weights[:, t, :], y[:, h * HALF:(h + 1) * HALF], start=True, stop=True)
                    last.then_inc(s[f"sc{t}_ps"], 1)

            def expert_set(l, g, parity):
                slots = [lane_slot(l, parity, j) for j in range(LANES)]
                most = pe.value_load(cnt[0:1, bass.ds(g, 1)], min_val=0, max_val=SEQ)
                n = pe.snap(g + l * SETS + 1)
                for j in range(LANES):
                    pe.wait_ge(gu_in[j], g * 32 + (l * SETS + 1) * 32)
                gate_up(first, g + (l * GATHERS + 1), hgT, slots)
                with pe.If(most <= SLOTS):
                    pe.sem_inc(slot_used, LANES)
                following = pe.snap(g + l * GATHERS + 2)
                gather(first, following)
                pe.wait_ge(x_moe, g + (l * SETS + 1))
                pe.wait_ge(x_more, g * MORE + (l * SETS * MORE + 1))
                transpose_weights(first, following, 6)
                transpose_act(first, n)

                def early(m):
                    pe.wait_ge(first["hg_d"], g + (l * GATHERS + 2))
                    pe.wait_ge(first["hg_a"], g + (l * GATHERS + 2))
                    gather(more, m)
                    transpose_weights(more, m, 7)
                    gate_up(more, m, hgT_more, slots)
                    pe.wait_ge(more["selwT_out"], m)
                    with pe.If(most <= 2 * SLOTS):
                        pe.sem_inc(slot_used, LANES)

                def late(m):
                    transpose_act(more, m)
                    pe.wait_ge(x_moe, g + (l * SETS + 2))
                    down(more)
                    pe.wait_ge(more["selwT_out"], m)
                    scatter(more, m, selwT_more)

                def whole(m, r):
                    pe.wait_ge(x_more, m)
                    gather(more, m)
                    transpose_weights(more, m, 7)
                    gate_up(more, m, hgT_more, slots)
                    transpose_act(more, m)
                    down(more)
                    pe.wait_ge(more["selwT_out"], m)
                    scatter(more, m, selwT_more)

                second_round_early(pe, g + l * SETS, most, early)
                for j in range(LANES):
                    pe.wait_ge(dn_in[j], g * 16 + (l * SETS + 1) * 16)
                down(first)
                pe.wait_ge(first["selwT_out"], g + (l * GATHERS + 2))
                scatter(first, n, selwT2[parity])
                further_rounds(pe, g + l * SETS, most, late, whole, PE_MORE)
                with pe.If(most > 2 * SLOTS):
                    pe.sem_inc(slot_used, LANES)
                pe.sem_inc(dn_used, 1)

            pe.wait_ge(ident_in, 16)
            for l in range(DEPTH):
                for t in range(TT):
                    transpose_x(2 * l, t)
                proj(l, 0)
                proj(l, 1)
                transpose_qk(l, 0)
                proj(l, 2)
                transpose_qk(l, 1)
                pe.wait_ge(qkT_d, l * 4 + 2)
                pe.wait_ge(qkT_a, l * 4 + 2)
                da_scores(l, 0)
                da_scores(l, 1)
                proj(l, 3)
                pe.wait_ge(da_max, l * 3 + 1)
                da_scores(l, 2)
                transpose_qk(l, 2)
                pe.wait_ge(proj_out, l * 12 + 8)
                da_transpose(l, 0)
                da_transpose(l, 1)
                transpose_qk(l, 3)
                pe.wait_ge(qkT_d, l * 4 + 4)
                pe.wait_ge(qkT_a, l * 4 + 4)
                sb_scores(l, 4, 5)
                pe.wait_ge(daT_out, l * 3 + 1)
                da_transpose(l, 2)
                sb_scores(l, 0, 1)
                proj_tile(l, 4, 0)
                pe.wait_ge(daT_out, l * 3 + 3)
                sb_scores(l, 2, 3)
                proj_tile(l, 4, 1)
                if l == 0:
                    pe.wait_ge(const_in, 16)
                cumulate(l, 4)
                cumulate(l, 5)
                proj_tile(l, 5, 0)
                cumulate(l, 0)
                cumulate(l, 1)
                proj_tile(l, 5, 1)
                cumulate(l, 2)
                cumulate(l, 3)
                pe.wait_ge(sb_arg, l * 6 + 2)
                pe.wait_ge(proj_out, l * 12 + 12)
                for t in range(TT):
                    for a in range(PAIRS):
                        for kt in range(t + 1):
                            p = aT[0][:, a, :] if t == 0 else aT[1 + a // 2][:, 2 * (a % 2) + kt, :]
                            MM(ps[DAO_BANK[t]][:, a * P:(a + 1) * P], p, v_sb[:, kt, 0, a * P:(a + 1) * P],
                               start=(kt == 0), stop=(kt == t))
                    if t == 0:
                        pe.wait_ge(sb_a, l * 6 + 6)
                    for hh in range(2 * PAIRS):
                        a, e = hh // 2, hh % 2
                        cols = slice(hh * HD, (hh + 1) * HD)
                        early = zm[:, 2 * (a // 2) + e, (a % 2) * SEQ:(a % 2 + 1) * SEQ]
                        MM(ps[SBO_BANK[t]][:, cols], early[:, t * P:(t + 1) * P], v_sb[:, 0, 1, cols],
                           start=True, stop=(t == 0))
                        if t == 1:
                            MM(ps[SBO_BANK[t]][:, cols], zm[:, 4 + e, a * P:(a + 1) * P], v_sb[:, 1, 1, cols],
                               start=False, stop=True)
                    pe.drain().then_inc(o_ps, 1)
                for t in range(TT):
                    pe.wait_ge(o_ready, l * TT + t + 1)
                    for k in range(KC):
                        last = TR(ps[OT_BANK[t][k // 4]][:, (k % 4) * P:(k % 4 + 1) * P], xn[:, t, k * P:(k + 1) * P], ident)
                        if k % 4 == 3:
                            last.then_inc(oT_ps, 1)
                    pe.wait_ge(oT_d, l * TT + t + 1)
                    pe.wait_ge(oT_a, l * TT + t + 1)
                    for h in range(2):
                        if t == 1 and h == 1:
                            transpose_x(2 * l + 1, 0)
                        i = len(ORDER) + h
                        pe.wait_ge(block_in[i], (l + 1) * 16)
                        w = block_of(l, i)
                        for k in range(KC):
                            last = MM(ps[OP_BANK[t][h]][:, :], hT[:, k, t * P:(t + 1) * P], w[:, k, :],
                                      start=(k == 0), stop=(k == KC - 1))
                        last.then_inc(oproj_ps, 1)
                        if t == 1:
                            pe.drain().then_inc(slot_used, 1)
                router(l, 0)
                transpose_x(2 * l + 1, 1)
                router(l, 1)
                ranks(l)
                pe.wait_ge(routed, l + 1)
                gather(first, l * GATHERS + 1)
                transpose_weights(first, l * GATHERS + 1, 6)
                pe.wait_ge(first["selwT_out"], l * GATHERS + 1)
                with pe.Fori(0, SETS // 2) as pair:
                    for parity in range(2):
                        expert_set(l, pe.snap(pair * 2 + parity), parity)


NAMES = ["x", "norm1_g", "w_in", "q_norm_g", "k_norm_g", "lambda_q1", "lambda_k1", "lambda_q2", "lambda_k2",
         "da_out_g", "sb_out_g", "w_out", "norm2_g", "w_router_group", "b_router_group", "w_router_expert",
         "b_router_expert", "w_gate", "w_up", "w_down"]


def kernel(**inputs):
    import concourse.bacc as bacc
    from concourse.bass_utils import run_bass_kernel_spmd

    nc = bacc.Bacc("TRN2", target_bir_lowering=False, num_devices=1)
    arrays = {"in_const": shape_constants()}
    arrays |= {f"in_{n}": np.ascontiguousarray(inputs[n]) for n in NAMES}
    aps = [nc.dram_tensor(n, a.shape, mybir.dt.from_np(a.dtype), kind="ExternalInput").ap() for n, a in arrays.items()]
    out = nc.dram_tensor("out_0", (1, SEQ, D), F32, kind="ExternalOutput").ap()
    decoder(nc, *aps, out)
    return run_bass_kernel_spmd(nc, [arrays], core_ids=[0]).results[0]["out_0"]
```

```python
import math
from contextlib import ExitStack

import concourse.bass as bass
import numpy as np
from concourse import mybir

F32 = mybir.dt.float32
I32 = mybir.dt.int32
ALU = mybir.AluOpType
ACT = mybir.ActivationFunctionType
AX = mybir.AxisListType

P = 128
D = 1024
SEQ = 256
DEPTH = 2
TT = SEQ // P
KC = D // P
HD = 64
PAIRS = 4
HALF = D // 2
GROUPS, PER_GROUP, EXPERTS = 4, 8, 32
FF = D // 4
FC = FF // P
LANES = 4
SLOTS = P // LANES
ROUNDS = SEQ // SLOTS
SETS = EXPERTS // LANES
ROPE = HD // 8
ROPE_THETA = 500000.0
EPS = 1e-6
SCALE = HD ** -0.5
NEG = -1e30
BIG = 64.0

DA_Q, DA_K, DA_V, SB_Q, SB_K, SB_V = range(6)
ORDER = [DA_Q, DA_K, SB_Q, SB_K, DA_V, SB_V]
BLOCKS = len(ORDER) + 2
SLOTS_W = 6
SIDE = SLOTS_W
SLOT = KC * HALF
UNITS = BLOCKS + EXPERTS


def block_slot(l, i):
    a, b = ((0, 1), (4, 5)) if l % 2 == 0 else ((4, 5), (0, 1))
    return (a + b + (2, 3) + a)[i]


def tile_number(i, t):
    return 2 * i + t + 1 if i < 4 else 2 * 4 + 2 * t + (i - 4) + 1


def lane_slot(l, g, j):
    if j < 2:
        return block_slot(l, 2 + j - 2 * (g % 2))
    return SIDE if j == 2 and g % 2 else j


def up_at(l, g, j):
    return (SLOTS_W + 1) * SLOT if j == 3 and g % 2 else lane_slot(l, g, j) * SLOT + SLOT // 2


def last_down_at(l, j):
    return (2 if j < 2 else block_slot(l, 3)) * SLOT + (j % 2) * (SLOT // 2)


SB_ORDER = [4, 5, 0, 1, 2, 3]
PROJ_BANK = [(4, 5), (6, 7), (4, 5), (6, 7), (4, 5), (4, 5)]
QKT_BANK = [(0, 1), (2, 3), (2, 3), (0, 1)]
DAS_BANK = [(0, 1), (2, 3), (0, 1)]
DAT_BANK = [6, 7, 6]
SB_BANK = [0, 1, 6, 7, 2, 3]
DAO_BANK = [2, 3]
SBO_BANK = [4, 5]
OT_BANK = [(0, 1), (6, 7)]
OP_BANK = [(2, 4), (3, 5)]
SC_BANK = [(4, 5), (6, 7)]

C_ID, C_GE, C_LT, C_ONE, C_MQ, C_MS, C_IOTA, C_REV, C_OFF, C_COS, C_SIN, C_END = np.cumsum(
    [0, P, P, P, P, 2 * P, 2 * P, P, EXPERTS, ROUNDS, TT * ROPE, TT * ROPE]).tolist()


def shape_constants():
    c = np.zeros((P, C_END), np.float32)
    i = np.arange(P)
    c[:, C_ID:C_GE] = np.eye(P)
    c[:, C_GE:C_LT] = i[:, None] >= i[None, :]
    c[:, C_LT:C_ONE] = i[:, None] < i[None, :]
    c[:, C_ONE:C_MQ] = 1.0
    c[:, C_MQ + P:C_MS] = np.where(i[None, :] <= i[:, None], 0.0, NEG)
    c[:, C_MS:C_MS + P] = np.where(i[:, None] < i[None, :], 0.0, NEG)
    c[:, C_IOTA:C_REV] = i % SLOTS + 1
    c[:, C_REV:C_OFF] = BIG - np.arange(EXPERTS)
    c[:, C_OFF:C_COS] = SLOTS * np.arange(ROUNDS)
    freq = (1.0 / (np.float32(ROPE_THETA) ** (np.arange(0, 2 * ROPE, 2, dtype=np.float32) / (2 * ROPE))))
    angle = np.arange(SEQ, dtype=np.float32)[:, None] * freq.astype(np.float32)[None, :]
    angle = angle.reshape(TT, P, ROPE).transpose(1, 0, 2).reshape(P, TT * ROPE).astype(np.float64)
    c[:, C_COS:C_SIN] = np.cos(angle)
    c[:, C_SIN:C_END] = np.sin(angle)
    return c


def decoder(nc, const, x, norm1_g, w_in, q_norm_g, k_norm_g, lambda_q1, lambda_k1, lambda_q2, lambda_k2,
            da_out_g, sb_out_g, w_out, norm2_g, w_router_group, b_router_group, w_router_expert,
            b_router_expert, w_gate, w_up, w_down, out):
    with ExitStack() as ctx:
        def sb(name, shape, dt=F32):
            return ctx.enter_context(nc.sbuf_tensor(name, shape, dt))

        def sem(name):
            return ctx.enter_context(nc.semaphore(name))

        wbuf = sb("wbuf", [P, (SLOTS_W + 1) * SLOT + SLOT // 2])
        dnbuf = sb("dnbuf", [P, LANES, FC * D])
        x_sb = sb("x_sb", [P, TT, D])
        xn = sb("xn", [P, TT, D])
        hTbuf = sb("hTbuf", [P, KC * SEQ])
        qkT = sb("qkT", [P, 4 * PAIRS * SEQ])
        cst = sb("cst", [P, C_END])
        g1T = sb("g1T", [P, KC])
        g2T = sb("g2T", [P, KC])
        g2 = sb("g2", [P, D])
        wr = sb("wr", [P, KC, GROUPS + EXPERTS])
        br = sb("br", [P, GROUPS + EXPERTS])
        qkg = sb("qkg", [P, 2, HD])
        dag = sb("dag", [P, 2 * HD])
        sbg = sb("sbg", [P, HD])
        lamv = sb("lamv", [P, 4, HD])
        lams = sb("lams", [P, 4])
        ssq = sb("ssq", [P, TT])
        rstd = sb("rstd", [P, TT])
        hss = sb("hss", [P, 2 * 16])
        hr = sb("hr", [P, 2 * 16])
        dmax = sb("dmax", [P, 3, 8])
        dsum = sb("dsum", [P, 3, 8])
        oss = sb("oss", [P, TT, 24])
        lg = sb("lg", [P, TT, GROUPS + EXPERTS])
        rs = sb("rs", [P, 8, TT])
        r4 = sb("r4", [P, 4, TT, GROUPS])
        rg4 = sb("rg4", [P, 4, TT * GROUPS])
        em = sb("em", [P, TT, EXPERTS])
        ev = sb("ev", [P, TT, EXPERTS])
        oh1 = sb("oh1", [P, TT, EXPERTS])
        oh2 = sb("oh2", [P, TT, EXPERTS])
        asg = sb("asg", [P, TT + 1, EXPERTS])
        wgt = sb("wgt", [P, TT, EXPERTS + LANES])
        pos = sb("pos", [P, TT, EXPERTS + LANES])
        posg = sb("posg", [P, TT, LANES])
        wgg = sb("wgg", [P, TT, LANES])
        cntf = sb("cntf", [P, SETS])
        cnt = sb("cnt", [P, SETS], I32)

        ident = cst[:, C_ID:C_GE]
        tri_ge = cst[:, C_GE:C_LT]
        tri_lt = cst[:, C_LT:C_ONE]
        ones = cst[:, C_ONE:C_MQ]

        def over(ap, n):
            return ap.unsqueeze(1).broadcast_to([P, n, ap.shape[1]])

        hT = hTbuf[:, :].rearrange("p (k t) -> p k t", k=KC)
        stage = wbuf[:, SIDE * SLOT:SIDE * SLOT + SLOT // 2].rearrange("p (b t c) -> p b t c", b=2, t=TT)
        v_sb = wbuf[:, SIDE * SLOT + SLOT // 2:(SIDE + 1) * SLOT]\
            .rearrange("p (t v c) -> p t v c", t=TT, v=2)
        scratch = dnbuf[:, :, :].rearrange("p a b -> p (a b)")
        s_da = scratch[:, 0:6 * HALF].rearrange("p (u e c) -> p u e c", u=3, e=2)
        zm = scratch[:, 6 * HALF:12 * HALF].rearrange("p (u c) -> p u c", u=6)
        aT = [s_da[:, u, 1, :].rearrange("p (b c) -> p b c", b=4) for u in range(3)]
        sp = [xn[:, w // 2, (w % 2) * HALF:(w % 2 + 1) * HALF] for w in range(4)] + \
             [scratch[:, (12 + w) * HALF:(13 + w) * HALF] for w in range(2)]
        sq = scratch[:, 6 * HALF:8 * HALF]
        rope = scratch[:, 0:4 * TT * 8 * ROPE].rearrange("p (n c) -> p n c", n=4)
        osq = scratch[:, 0:4 * HALF].rearrange("p (u c) -> p u c", u=4)
        qk = qkT[:, :].rearrange("p (i a t) -> p i a t", i=4, a=PAIRS)
        at = [0]

        def take(n):
            at[0] += n
            return qkT[:, at[0] - n:at[0]]
        hgT = take(KC * P).rearrange("p (k s) -> p k s", k=KC)
        y = take(D)
        eg, rg, tg = take(FF), take(FF), take(FF)
        act_sb = take(FF)
        actT = take(FF).rearrange("p (c s) -> p c s", c=FC)
        sel = take(TT * P).rearrange("p (t s) -> p t s", t=TT)
        selw = take(TT * P).rearrange("p (t s) -> p t s", t=TT)
        selwT2 = [take(TT * P).rearrange("p (t s) -> p t s", t=TT),
                  hTbuf[:, KC * P:KC * P + TT * P].rearrange("p (t s) -> p t s", t=TT)]
        hgT_more = hTbuf[:, 0:KC * P].rearrange("p (k s) -> p k s", k=KC)
        selwT_more, sel_more, selw_more = [hTbuf[:, (KC + n * TT) * P:(KC + (n + 1) * TT) * P]
                                           .rearrange("p (t s) -> p t s", t=TT) for n in (1, 2, 3)]

        ps = [ctx.enter_context(nc.psum_tensor(f"bank{i}", [P, HALF], F32)) for i in range(8)]

        zeros_ready = sem("zeros_ready")
        ident_in, const_in = sem("ident_in"), sem("const_in")
        x_in = [sem(f"x_in{t}") for t in range(TT)]
        g1_in = [sem(f"g1_in{l}") for l in range(DEPTH)]
        gains_in = [sem(f"gains_in{l}") for l in range(DEPTH)]
        par_in = [sem(f"par_in{l}") for l in range(DEPTH)]
        block_in = [sem(f"block_in{i}") for i in range(BLOCKS)]
        block0_rest_in = sem("block0_rest_in")
        gu_in = [[sem(f"gu_in{p}{j}") for j in range(LANES)] for p in range(2)]
        dn_in = [sem(f"dn_in{j}") for j in range(LANES)]
        dn_last_in = [sem(f"dn_last_in{j}") for j in range(LANES)]
        out_done = sem("out_done")
        norm_r = sem("norm_r")
        hT_ps, hT_d, hT_a = sem("hT_ps"), sem("hT_d"), sem("hT_a")
        proj_ps, proj_out, slot_used = sem("proj_ps"), sem("proj_out"), sem("slot_used")
        qk_ss, qk_r, qk_normed = sem("qk_ss"), sem("qk_r"), sem("qk_normed")
        qkT_ps, qkT_d, qkT_a = sem("qkT_ps"), sem("qkT_d"), sem("qkT_a")
        lam_dot, lam_exp = sem("lam_dot"), sem("lam_exp")
        da_ps, da_max, da_exp, da_mix = sem("da_ps"), sem("da_max"), sem("da_exp"), sem("da_mix")
        daT_ps, daT_out, o_ps = sem("daT_ps"), sem("daT_out"), sem("o_ps")
        sb_ps, sb_abs, sb_ln, sb_sp = sem("sb_ps"), sem("sb_abs"), sem("sb_ln"), sem("sb_sp")
        sb_cum, sb_arg, sb_a = sem("sb_cum"), sem("sb_arg"), sem("sb_a")
        o_sq, o_ss, o_r, o_ready = sem("o_sq"), sem("o_ss"), sem("o_r"), sem("o_ready")
        oT_ps, oT_d, oT_a = sem("oT_ps"), sem("oT_d"), sem("oT_a")
        oproj_ps, x_attn = sem("oproj_ps"), sem("x_attn")
        lg_ps, rt_diff, rt_exp, rt_asg = sem("lg_ps"), sem("rt_diff"), sem("rt_exp"), sem("rt_asg")
        pos_ps, routed = sem("pos_ps"), sem("routed")
        STEPS = ["sel_ready", "selw_ready", "gathered", "selwT_ps", "hg_d", "hg_a", "selwT_out", "gu_ps", "gate_exp",
                 "act_out", "actT_ps", "actT_out", "dn0_ps", "dn1_ps", "y_d", "y_a", "sc0_ps", "sc1_ps"]
        first = {n: sem(n) for n in STEPS}
        more = {n: sem("more_" + n) for n in STEPS}
        x_moe, x_more, x_done = sem("x_moe"), sem("x_more"), sem("x_done")
        x_moe0 = sem("x_moe0")
        dn_used = sem("dn_used")
        PE_MORE = [more[n] for n in ("gathered", "selwT_ps", "gu_ps", "actT_ps", "dn0_ps", "dn1_ps", "sc0_ps", "sc1_ps")]
        ACT_MORE = [more[n] for n in ("hg_a", "gate_exp", "y_a")]
        DVE_MORE = [more[n] for n in ("sel_ready", "selw_ready", "hg_d", "selwT_out", "act_out", "actT_out", "y_d")] + [x_more]

        def bcast(v, n):
            return v.unsqueeze(0).broadcast_to([P, n])

        def gain1(l):
            return norm1_g[l].rearrange("(p k) -> p k", k=KC)

        def gains(l):
            yield qkg[:, 0, :], bcast(q_norm_g[l], HD)
            yield qkg[:, 1, :], bcast(k_norm_g[l], HD)
            for n, v in enumerate((lambda_q1, lambda_k1, lambda_q2, lambda_k2)):
                yield lamv[:, n, :], bcast(v[l], HD)
        N_GAINS = 6 * 16

        def params(l):
            yield dag[:, :], bcast(da_out_g[l], 2 * HD)
            yield sbg[:, :], bcast(sb_out_g[l], HD)
            yield g2[:, :], bcast(norm2_g[l], D)
            yield g2T[:, :], norm2_g[l].rearrange("(p k) -> p k", k=KC)
            yield wr[:, :, 0:GROUPS], w_router_group[l].rearrange("(p k) n -> p k n", k=KC)
            yield wr[:, :, GROUPS:], w_router_expert[l].rearrange("(p k) n -> p k n", k=KC)
            yield br[:, 0:GROUPS], bcast(b_router_group[l], GROUPS)
            yield br[:, GROUPS:], bcast(b_router_expert[l], EXPERTS)
        N_PAR = 8 * 16

        w_gate_e = w_gate.rearrange("l e (p k) f -> (l e) p (k f)", k=KC)
        w_up_e = w_up.rearrange("l e (p k) f -> (l e) p (k f)", k=KC)
        w_down_e = w_down.rearrange("l e (p c) d -> (l e) p (c d)", c=FC)

        MORE = ROUNDS - 1
        GATHERS = SETS + 1

        def second_round_early(eng, n_set, most, early):
            with eng.If(most > SLOTS):
                early(eng.snap(n_set * MORE + 1))

        def further_rounds(eng, n_set, most, late, whole, owed):
            base = eng.snap(n_set * MORE)
            with eng.If(most > SLOTS):
                late(eng.snap(base + 1))
                with eng.If(most > 2 * SLOTS):
                    with eng.Fori(2, ROUNDS) as r:
                        with eng.If(most > r * SLOTS):
                            whole(eng.snap(base + r), r)
                        with eng.Else():
                            eng.drain()
                            for s in owed:
                                eng.sem_inc(s, 1)
                with eng.Else():
                    eng.drain()
                    for s in owed:
                        eng.sem_inc(s, MORE - 1)
            with eng.Else():
                eng.drain()
                for s in owed:
                    eng.sem_inc(s, MORE)

        block = ctx.enter_context(nc.Block())

        @block.sync
        def _(sp_):
            def load_block(l, i):
                free = l * UNITS + (-LANES, -LANES, 0, 0, 0, 0, 1, 2)[i]
                if free > 0:
                    sp_.wait_ge(slot_used, free)
                if l > 0 and i in (1, 4):
                    sp_.wait_ge(dn_used, l * SETS)
                w, c = (w_in, ORDER[i] * HALF) if i < len(ORDER) else (w_out, (i - len(ORDER)) * HALF)
                dst = wbuf[:, block_slot(l, i) * SLOT:(block_slot(l, i) + 1) * SLOT].rearrange("p (k c) -> p k c", k=KC)
                src = w[l, :, c:c + HALF].rearrange("(p k) c -> p k c" if i < len(ORDER) else "(k p) c -> p k c", p=P)
                if i == 0:
                    sp_.dma_start(dst[:, 0:KC // 2, :], src[:, 0:KC // 2, :]).then_inc(block_in[0], 16)
                    sp_.dma_start(dst[:, KC // 2:, :], src[:, KC // 2:, :]).then_inc(block0_rest_in, 16)
                else:
                    sp_.dma_start(dst, src).then_inc(block_in[i], 16)

            def load_gate(l, g, parity, j):
                at = lane_slot(l, parity, j) * SLOT
                sp_.dma_start(wbuf[:, at:at + SLOT // 2], w_gate_e[g * LANES + (l * EXPERTS + j)]).then_inc(gu_in[parity][j], 16)

            def load_up(l, g, parity, j):
                at = up_at(l, parity, j)
                sp_.dma_start(wbuf[:, at:at + SLOT // 2], w_up_e[g * LANES + (l * EXPERTS + j)]).then_inc(gu_in[parity][j], 16)

            def load_gu(l, g, parity, j):
                load_gate(l, g, parity, j)
                load_up(l, g, parity, j)

            LAST = SETS - 1

            def load_rest(l, g, parity):
                sp_.wait_ge(slot_used, g * LANES + (l * UNITS + BLOCKS))
                load_gate(l, g, parity, 3)
                if g is LAST:
                    if l + 1 < DEPTH:
                        load_block(l + 1, 0)
                else:
                    load_gu(l, g + 1, 1 - parity, 0)
                if g is LAST:
                    for j in range(LANES):
                        at = last_down_at(l, j)
                        sp_.dma_start(wbuf[:, at:at + SLOT // 2], w_down_e[LAST * LANES + l * EXPERTS + j])\
                           .then_inc(dn_last_in[j], 16)
                else:
                    sp_.wait_ge(dn_used, g + l * SETS)
                    for j in range(LANES):
                        load_dn(l, g, j)
                    load_gu(l, g + 1, 1 - parity, 1)
                    load_gu(l, g + 1, 1 - parity, 2)
                    load_up(l, g + 1, 1 - parity, 3)

            def load_dn(l, g, j):
                sp_.dma_start(dnbuf[:, j, :], w_down_e[g * LANES + (l * EXPERTS + j)]).then_inc(dn_in[j], 16)

            sp_.dma_start(x_sb[:, 0, :], x[0, 0:P, :]).then_inc(x_in[0], 16)
            sp_.dma_start(ident, const[:, C_ID:C_GE]).then_inc(ident_in, 16)
            sp_.dma_start(g1T[:, :], gain1(0)).then_inc(g1_in[0], 16)
            sp_.dma_start(x_sb[:, 1, :], x[0, P:2 * P, :]).then_inc(x_in[1], 16)
            for l in range(DEPTH):
                for i in range(BLOCKS):
                    if l == 0 or i > 0:
                        load_block(l, i)
                    if l == 0 and i == 1:
                        sp_.dma_start(cst[:, C_GE:], const[:, C_GE:]).then_inc(const_in, 16)
                        for dst, src in gains(0):
                            sp_.dma_start(dst, src).then_inc(gains_in[0], 16)
                        for dst, src in params(0):
                            sp_.dma_start(dst, src).then_inc(par_in[0], 16)
                for j in range(LANES):
                    sp_.wait_ge(slot_used, l * UNITS + 3 + j)
                    load_gu(l, 0, 0, j)
                sp_.wait_ge(o_ready, (l + 1) * TT)
                for j in range(LANES):
                    load_dn(l, 0, j)
                load_gu(l, 1, 1, 2)
                load_up(l, 1, 1, 3)
                for j in range(2):
                    sp_.wait_ge(slot_used, l * UNITS + BLOCKS - 1 + j)
                    load_gu(l, 1, 1, j)
                with sp_.Fori(0, SETS // 2 - 1) as h:
                    load_rest(l, sp_.snap(h * 2 + 1), 1)
                    load_rest(l, sp_.snap(h * 2 + 2), 0)
                load_rest(l, LAST, 1)
            sp_.wait_ge(x_done, DEPTH)
            sp_.dma_start(out[0].rearrange("(t p) d -> p t d", p=P), x_sb[:, :, :]).then_inc(out_done, 16)
            sp_.wait_ge(out_done, 16)

        @block.gpsimd
        def _(pool):
            for l in range(1, DEPTH):
                pool.wait_ge(routed, l)
                nc.gpsimd.dma_start(g1T[:, :], gain1(l)).then_inc(g1_in[l], 16)
                for dst, src in gains(l):
                    nc.gpsimd.dma_start(dst, src).then_inc(gains_in[l], 16)
                pool.wait_ge(x_done, l)
                for dst, src in params(l):
                    nc.gpsimd.dma_start(dst, src).then_inc(par_in[l], 16)

        @block.scalar
        def _(act):
            act.preload_act_table_set("natural_log_exp_and_others")

            def scales(out_ap, in_ap, width):
                nc.scalar.activation(out_ap, in_ap, ACT.Ln, bias=EPS, scale=1.0 / width)
                act.drain()
                return nc.scalar.activation(out_ap, out_ap, ACT.Exp, scale=-0.5)

            def norm(l, t):
                nc.scalar.activation(y, x_sb[:, t, :], ACT.Square, accum_out=ssq[:, t:t + 1])
                act.drain()
                scales(rstd[:, t:t + 1], ssq[:, t:t + 1], D)
                act.drain().then_inc(norm_r, 1)

            def hT_half(n, t, gain):
                act.wait_ge(hT_ps, n * 2 * TT + 2 * t + 2)
                for k in range(4):
                    last = nc.scalar.activation(hT[:, 4 + k, t * P:(t + 1) * P], ps[2 * t + 1][:, k * P:(k + 1) * P],
                                                ACT.Copy, scale=gain[:, 4 + k:5 + k])
                last.then_inc(hT_a, 1)

            def proj_tile(l, i, t):
                act.wait_ge(proj_ps, l * 12 + tile_number(i, t))
                if t == TT - 1:
                    act.sem_inc(slot_used, 1)
                if i in (2, 3):
                    act.wait_ge(qkT_ps, l * 8 + 2 * (i - 2) + 2)
                dst = stage[:, i % 2, t, :] if i < 4 else v_sb[:, t, i - 4, :]
                nc.scalar.activation(dst, ps[PROJ_BANK[i][t]][:, :], ACT.Copy, scale=rstd[:, t:t + 1]).then_inc(proj_out, 1)

            def proj(l, i):
                for t in range(TT):
                    proj_tile(l, i, t)

            def qk_scale(l, i):
                act.wait_ge(qk_ss, l * 2 + i + 1)
                scales(hr[:, i * 16:i * 16 + 16], hss[:, i * 16:i * 16 + 16], HD).then_inc(qk_r, 1)

            def qkT_half(l, i):
                act.wait_ge(qkT_ps, l * 8 + 2 * i + 2)
                nc.scalar.copy(qk[:, i, :, P:2 * P], ps[QKT_BANK[i][1]][:, :].rearrange("p (a c) -> p a c", a=PAIRS))\
                  .then_inc(qkT_a, 1)

            def softmax_exp(l, u):
                act.wait_ge(da_max, l * 3 + u + 1)
                keys = P if u == 0 else 2 * P
                heads = HALF // keys
                for e in range(2):
                    for h in range(heads):
                        c = e * heads + h
                        s = s_da[:, u, e, h * keys:(h + 1) * keys]
                        last = nc.scalar.activation(s, s, ACT.Exp, bias=dmax[:, u, c:c + 1],
                                                    accum_out=dsum[:, u, c:c + 1])
                act.drain().then_inc(da_exp, 1)

            def softplus_ln(l, ws):
                for w in ws:
                    n = SB_ORDER.index(w)
                    act.wait_ge(sb_abs, l * 6 + n + 1)
                    nc.scalar.activation(sp[w], sp[w], ACT.Exp)
                act.drain()
                for w in ws:
                    nc.scalar.activation(sp[w], sp[w], ACT.Ln, bias=1.0).then_inc(sb_ln, 1)

            def daT_copy(l, u):
                act.wait_ge(daT_ps, l * 3 + u + 1)
                nc.scalar.copy(aT[u], ps[DAT_BANK[u]][:, :].rearrange("p (b c) -> p b c", b=4)).then_inc(daT_out, 1)

            def break_exp(l, w):
                act.wait_ge(sb_arg, l * 6 + SB_ORDER.index(w) + 1)
                nc.scalar.activation(zm[:, w, :], zm[:, w, :], ACT.Exp).then_inc(sb_a, 1)

            def oT_half(l, t):
                act.wait_ge(oT_ps, l * 4 + 2 * t + 2)
                nc.scalar.copy(hT[:, 4:8, t * P:(t + 1) * P],
                               ps[OT_BANK[t][1]][:, :].rearrange("p (k c) -> p k c", k=4)).then_inc(oT_a, 1)

            def gather_copy(s, n, dst):
                act.wait_ge(s["gathered"], n)
                nc.scalar.copy(dst[:, 4:8, :], ps[1][:, :].rearrange("p (k s) -> p k s", k=4)).then_inc(s["hg_a"], 1)

            def gate(s, n):
                act.wait_ge(s["gu_ps"], n)
                nc.scalar.activation(eg, ps[2][:, 0:FF], ACT.Exp, scale=-1.0).then_inc(s["gate_exp"], 1)

            def y_copy(s, n):
                act.wait_ge(s["dn1_ps"], n)
                nc.scalar.copy(y[:, HALF:], ps[5][:, :]).then_inc(s["y_a"], 1)

            def early(n):
                gather_copy(more, n, hgT_more)
                gate(more, n)

            def late(n):
                y_copy(more, n)

            def whole(n, r):
                early(n)
                late(n)

            for l in range(DEPTH):
                act.wait_ge(g1_in[l], 16)
                for t in range(TT):
                    hT_half(2 * l, t, g1T)
                for t in range(TT):
                    if l == 0:
                        act.wait_ge(x_in[t], 16)
                    else:
                        act.wait_ge(x_done, l)
                    norm(l, t)
                act.wait_ge(lam_dot, l + 1)
                nc.scalar.activation(lams[:, 2:4], lams[:, 0:2], ACT.Exp).then_inc(lam_exp, 1)
                proj(l, 0)
                qk_scale(l, 0)
                proj(l, 1)
                qk_scale(l, 1)
                qkT_half(l, 0)
                proj(l, 2)
                qkT_half(l, 1)
                proj_tile(l, 3, 0)
                softmax_exp(l, 0)
                softmax_exp(l, 1)
                proj_tile(l, 3, 1)
                qkT_half(l, 2)
                qkT_half(l, 3)
                daT_copy(l, 0)
                daT_copy(l, 1)
                softmax_exp(l, 2)
                softplus_ln(l, (4, 5))
                softplus_ln(l, (0, 1))
                proj_tile(l, 4, 0)
                daT_copy(l, 2)
                softplus_ln(l, (2, 3))
                break_exp(l, 4)
                break_exp(l, 5)
                proj_tile(l, 5, 0)
                for w in range(4):
                    break_exp(l, w)
                proj_tile(l, 4, 1)
                for t in range(TT):
                    act.wait_ge(o_ps, l * TT + t + 1)
                    nc.scalar.activation(osq[:, 2 * t, :], ps[DAO_BANK[t]][:, :], ACT.Square)
                    nc.scalar.activation(osq[:, 2 * t + 1, :], ps[SBO_BANK[t]][:, :], ACT.Square)
                    act.drain().then_inc(o_sq, 1)
                    act.wait_ge(o_ss, l * TT + t + 1)
                    scales(oss[:, t, 12:16], oss[:, t, 0:4], 2 * HD)
                    scales(oss[:, t, 16:24], oss[:, t, 4:12], HD)
                    act.drain().then_inc(o_r, 1)
                    if t == 0:
                        proj_tile(l, 5, 1)
                        oT_half(l, 0)
                oT_half(l, 1)
                act.wait_ge(par_in[l], N_PAR)
                for t in range(TT):
                    act.wait_ge(x_attn, l * 2 * TT + 2 * (t + 1))
                    norm(l, t)
                    hT_half(2 * l + 1, t, g2T)
                act.wait_ge(rt_diff, 2 * l + 1)
                nc.scalar.activation(r4[:, 1], r4[:, 0], ACT.Exp).then_inc(rt_exp, 1)
                act.wait_ge(rt_diff, 2 * l + 2)
                nc.scalar.activation(rs[:, 5, :], rs[:, 4, :], ACT.Exp).then_inc(rt_exp, 1)
                gather_copy(first, l * GATHERS + 1, hgT)
                act.wait_ge(routed, l + 1)
                with act.Fori(0, SETS) as g:
                    most = act.value_load(cnt[0:1, bass.ds(g, 1)], min_val=0, max_val=SEQ)
                    gate(first, act.snap(g + l * SETS + 1))
                    gather_copy(first, act.snap(g + l * GATHERS + 2), hgT)
                    second_round_early(act, g + l * SETS, most, early)
                    y_copy(first, act.snap(g + l * SETS + 1))
                    further_rounds(act, g + l * SETS, most, late, whole, ACT_MORE)

        @block.vector
        def _(dve):
            V = nc.vector
            gap = dve.drain

            def hT_half(n, t, gain):
                dve.wait_ge(hT_ps, n * 2 * TT + 2 * t + 1)
                V.tensor_tensor(hT[:, 0:4, t * P:(t + 1) * P], ps[2 * t][:, :].rearrange("p (k c) -> p k c", k=4),
                                gain[:, 0:4].unsqueeze(2).broadcast_to([P, 4, P]), ALU.mult).then_inc(hT_d, 1)

            def normed(l, t):
                dve.wait_ge(norm_r, 4 * l + 2 + t + 1)
                V.scalar_tensor_tensor(xn[:, t, :].rearrange("p (k c) -> p c k", k=KC),
                                       x_sb[:, t, :].rearrange("p (c k) -> p c k", k=KC), rstd[:, t:t + 1],
                                       g2[:, :].rearrange("p (c k) -> p c k", k=KC), ALU.mult, ALU.mult)

            def qk_norm(l, i):
                b = stage[:, i, :, :]
                rows = b.rearrange("p t c -> p (t c)")
                heads = rows.rearrange("p (h c) -> p h c", c=HD)
                dve.wait_ge(proj_out, l * 12 + 2 * i + 2)
                V.tensor_tensor(sq, rows, rows, ALU.mult)
                gap()
                V.tensor_reduce(hss[:, i * 16:i * 16 + 16], sq.rearrange("p (h c) -> p h c", c=HD),
                                AX.X, ALU.add).then_inc(qk_ss, 1)
                dve.wait_ge(qk_r, l * 2 + i + 1)
                V.tensor_tensor(heads, heads, hr[:, i * 16:i * 16 + 16].unsqueeze(2).broadcast_to([P, 16, HD]), ALU.mult)
                gap()
                V.tensor_tensor(heads, heads, over(qkg[:, i, :], 16), ALU.mult)
                gap()
                for t in range(TT):
                    h = b[:, t, :].rearrange("p (h c) -> p h c", c=HD)
                    first, second = h[:, :, 0:ROPE], h[:, :, ROPE:2 * ROPE]
                    cos = over(cst[:, C_COS + t * ROPE:C_COS + (t + 1) * ROPE], 8)
                    sin = over(cst[:, C_SIN + t * ROPE:C_SIN + (t + 1) * ROPE], 8)
                    part = [rope[:, n, t * 8 * ROPE:(t + 1) * 8 * ROPE].rearrange("p (h c) -> p h c", c=ROPE) for n in range(4)]
                    V.tensor_tensor(part[0], first, cos, ALU.mult)
                    V.tensor_tensor(part[1], second, sin, ALU.mult)
                    V.tensor_tensor(part[2], second, cos, ALU.mult)
                    V.tensor_tensor(part[3], first, sin, ALU.mult)
                gap()
                for t in range(TT):
                    h = b[:, t, :].rearrange("p (h c) -> p h c", c=HD)
                    part = [rope[:, n, t * 8 * ROPE:(t + 1) * 8 * ROPE].rearrange("p (h c) -> p h c", c=ROPE) for n in range(4)]
                    V.tensor_tensor(h[:, :, 0:ROPE], part[0], part[1], ALU.subtract)
                    last = V.tensor_tensor(h[:, :, ROPE:2 * ROPE], part[2], part[3], ALU.add)
                gap().then_inc(qk_normed, 1)

            def qkT_half(l, i):
                dve.wait_ge(qkT_ps, l * 8 + 2 * i + 1)
                V.tensor_copy(qk[:, i, :, 0:P], ps[QKT_BANK[i][0]][:, :].rearrange("p (a c) -> p a c", a=PAIRS))\
                 .then_inc(qkT_d, 1)

            def da_scores(l, u):
                keys = P if u == 0 else 2 * P
                heads = HALF // keys
                mask = cst[:, C_MQ + (P if u == 0 else 0):C_MQ + 2 * P]
                dve.wait_ge(da_ps, (l * 3 + u + 1) * 2)
                for e in range(2):
                    V.scalar_tensor_tensor(s_da[:, u, e, :].rearrange("p (h c) -> p h c", h=heads),
                                           ps[DAS_BANK[u][e]][:, :].rearrange("p (h c) -> p h c", h=heads),
                                           SCALE, over(mask, heads), ALU.mult, ALU.add)
                gap()
                V.tensor_reduce(dmax[:, u, 0:2 * heads], s_da[:, u].rearrange("p e (h c) -> p (e h) c", h=heads),
                                AX.X, ALU.max, negate=True).then_inc(da_max, 1)

            def da_mix_(l, u):
                keys = P if u == 0 else 2 * P
                heads = HALF // keys
                dve.wait_ge(da_exp, l * 3 + u + 1)
                V.reciprocal(dsum[:, u, 0:2 * heads], dsum[:, u, 0:2 * heads])
                gap()
                V.tensor_scalar(dsum[:, u, heads:2 * heads], dsum[:, u, heads:2 * heads], lams[:, 0:1], None, ALU.mult)
                gap()
                for h in range(heads):
                    c = slice(h * keys, (h + 1) * keys)
                    V.tensor_scalar(s_da[:, u, 0, c], s_da[:, u, 0, c], dsum[:, u, h:h + 1], None, ALU.mult)
                gap()
                for h in range(heads):
                    c = slice(h * keys, (h + 1) * keys)
                    V.scalar_tensor_tensor(s_da[:, u, 0, c], s_da[:, u, 1, c], dsum[:, u, heads + h:heads + h + 1],
                                           s_da[:, u, 0, c], ALU.mult, ALU.add)
                gap().then_inc(da_mix, 1)

            def sb_scores(l, ws):
                for w in ws:
                    heads = 4 if w >= 4 else 2
                    mask = cst[:, C_MS:C_MS + (P if w >= 4 else 2 * P)]
                    dve.wait_ge(sb_ps, l * 6 + SB_ORDER.index(w) // 2 * 2 + 2)
                    V.scalar_tensor_tensor(zm[:, w, :].rearrange("p (h c) -> p h c", h=heads),
                                           ps[SB_BANK[w]][:, :].rearrange("p (h c) -> p h c", h=heads),
                                           SCALE, over(mask, heads), ALU.mult, ALU.add)
                gap()
                for w in ws:
                    V.scalar_tensor_tensor(sp[w], zm[:, w, :], -1.0, zm[:, w, :], ALU.mult, ALU.min).then_inc(sb_abs, 1)

            def sb_softplus(l, ws):
                for w in ws:
                    dve.wait_ge(sb_ln, l * 6 + SB_ORDER.index(w) + 1)
                    V.scalar_tensor_tensor(sp[w], zm[:, w, :], 0.0, sp[w], ALU.max, ALU.add).then_inc(sb_sp, 1)

            def sb_argument(l, w):
                dve.wait_ge(sb_cum, l * 6 + SB_ORDER.index(w) + 1)
                V.tensor_tensor(zm[:, w, :], zm[:, w, :], ps[SB_BANK[w]][:, :], ALU.subtract).then_inc(sb_arg, 1)

            def oT_half(l, t):
                dve.wait_ge(oT_ps, l * 4 + 2 * t + 1)
                V.tensor_copy(hT[:, 0:4, t * P:(t + 1) * P],
                              ps[OT_BANK[t][0]][:, :].rearrange("p (k c) -> p k c", k=4)).then_inc(oT_d, 1)

            slots_shape = [P, LANES, SLOTS]

            def select_slots(s, rank, sel):
                for t in range(TT):
                    V.tensor_tensor(sel[:, t, :].rearrange("p (j s) -> p j s", j=LANES),
                                    cst[:, C_IOTA:C_REV].rearrange("p (j s) -> p j s", j=LANES),
                                    rank[t].unsqueeze(2).broadcast_to(slots_shape), ALU.is_equal)
                gap().then_inc(s["sel_ready"], 1)

            def select_weights(s, weight, sel, selw):
                for t in range(TT):
                    V.tensor_tensor(selw[:, t, :].rearrange("p (j s) -> p j s", j=LANES),
                                    sel[:, t, :].rearrange("p (j s) -> p j s", j=LANES),
                                    weight[t].unsqueeze(2).broadcast_to(slots_shape), ALU.mult)
                gap().then_inc(s["selw_ready"], 1)

            def select(s, g, r, sel, selw):
                for t in range(TT):
                    V.tensor_copy(posg[:, t, :], pos[:, t, bass.ds(g * LANES, LANES)])
                    V.tensor_copy(wgg[:, t, :], wgt[:, t, bass.ds(g * LANES, LANES)])
                gap()
                if r is not None:
                    V.tensor_tensor(posg[:, :, :], posg[:, :, :],
                                    cst[:, bass.ds(r + C_OFF, 1)].unsqueeze(2).broadcast_to([P, TT, LANES]), ALU.subtract)
                    gap()
                select_slots(s, [posg[:, t, :] for t in range(TT)], sel)
                select_weights(s, [wgg[:, t, :] for t in range(TT)], sel, selw)

            def gather_copy(s, n, dst, dst_w, bank):
                dve.wait_ge(s["gathered"], n)
                V.tensor_copy(dst[:, 0:4, :], ps[0][:, :].rearrange("p (k s) -> p k s", k=4)).then_inc(s["hg_d"], 1)
                dve.wait_ge(s["selwT_ps"], n)
                V.tensor_copy(dst_w.rearrange("p t s -> p (t s)"), ps[bank][:, 0:TT * P]).then_inc(s["selwT_out"], 1)

            def activate(s, n):
                dve.wait_ge(s["gate_exp"], n)
                V.tensor_scalar(rg, eg, 1.0, None, ALU.add)
                gap()
                V.reciprocal(rg, rg)
                gap()
                V.tensor_tensor(tg, ps[2][:, 0:FF], rg, ALU.mult)
                gap()
                V.tensor_tensor(act_sb.rearrange("p (c f) -> p f c", c=FC),
                                ps[2][:, FF:2 * FF].rearrange("p (f c) -> p f c", c=FC),
                                tg.rearrange("p (f c) -> p f c", c=FC), ALU.mult).then_inc(s["act_out"], 1)

            def act_copy(s, n):
                dve.wait_ge(s["actT_ps"], n)
                V.tensor_copy(actT.rearrange("p c s -> p (c s)"), ps[3][:, 0:FF]).then_inc(s["actT_out"], 1)

            def y_copy(s, n):
                dve.wait_ge(s["dn0_ps"], n)
                V.tensor_copy(y[:, 0:HALF], ps[4][:, :]).then_inc(s["y_d"], 1)

            def into_x(s, n, done):
                for t in range(TT):
                    dve.wait_ge(s[f"sc{t}_ps"], n)
                    for h in range(2):
                        c = slice(h * HALF, (h + 1) * HALF)
                        last = V.tensor_tensor(x_sb[:, t, c], x_sb[:, t, c], ps[SC_BANK[t][h]][:, :], ALU.add)
                    if t == 0 and s is first:
                        last.then_inc(x_moe0, 1)
                gap().then_inc(done, 1)

            def expert_set(l, g, parity):
                most = dve.value_load(cnt[0:1, bass.ds(g, 1)], min_val=0, max_val=SEQ)
                dve.wait_ge(first["selwT_ps"], g + (l * GATHERS + 1))
                select(first, g + 1, None, sel, selw)
                with dve.If(most > SLOTS):
                    select(more, g, 1, sel_more, selw_more)
                n = dve.snap(g + l * SETS + 1)
                activate(first, n)
                act_copy(first, n)
                gather_copy(first, dve.snap(g + l * GATHERS + 2), hgT, selwT2[1 - parity], 6)

                def early(m):
                    gather_copy(more, m, hgT_more, selwT_more, 7)
                    activate(more, m)

                def late(m):
                    y_copy(more, m)
                    into_x(more, m, x_more)

                def whole(m, r):
                    select(more, g, r, sel_more, selw_more)
                    early(m)
                    act_copy(more, m)
                    late(m)
                second_round_early(dve, g + l * SETS, most, early)
                y_copy(first, n)
                with dve.If(most > SLOTS):
                    dve.wait_ge(first["dn1_ps"], n)
                    act_copy(more, dve.snap(g * MORE + (l * SETS * MORE + 1)))
                into_x(first, n, x_moe)
                further_rounds(dve, g + l * SETS, most, late, whole, DVE_MORE)

            dve.sem_inc(x_moe, 1)
            dve.sem_inc(x_more, 1)
            V.memset(xn[:, 0, 0:P], 0.0).then_inc(zeros_ready, 1)
            V.memset(pos[:, :, EXPERTS:], 0.0)
            V.memset(wgt[:, :, EXPERTS:], 0.0)
            for l in range(DEPTH):
                lam_init = 0.8 - 0.6 * math.exp(-0.3 * l)
                dve.wait_ge(g1_in[l], 16)
                for t in range(TT):
                    hT_half(2 * l, t, g1T)
                if l == 0:
                    dve.wait_ge(const_in, 16)
                dve.wait_ge(gains_in[l], N_GAINS)
                prod = sq[:, 0:2 * HD].rearrange("p (n c) -> p n c", n=2)
                V.tensor_tensor(prod, lamv[:, 0:4:2, :], lamv[:, 1:4:2, :], ALU.mult)
                gap()
                V.tensor_reduce(lams[:, 0:2], prod, AX.X, ALU.add).then_inc(lam_dot, 1)
                dve.wait_ge(lam_exp, l + 1)
                V.tensor_scalar(lams[:, 0:1], lams[:, 3:4], lams[:, 2:3], -lam_init, ALU.subtract, ALU.add)
                gap()
                qk_norm(l, 0)
                qk_norm(l, 1)
                qkT_half(l, 0)
                qkT_half(l, 1)
                da_scores(l, 0)
                da_scores(l, 1)
                da_mix_(l, 0)
                da_mix_(l, 1)
                da_scores(l, 2)
                qkT_half(l, 2)
                qkT_half(l, 3)
                sb_scores(l, (4, 5))
                da_mix_(l, 2)
                sb_scores(l, (0, 1))
                sb_softplus(l, (4, 5))
                sb_scores(l, (2, 3))
                sb_softplus(l, (0, 1))
                sb_softplus(l, (2, 3))
                for w in SB_ORDER:
                    sb_argument(l, w)
                dve.wait_ge(par_in[l], N_PAR)
                for t in range(TT):
                    dve.wait_ge(o_sq, l * TT + t + 1)
                    V.tensor_reduce(oss[:, t, 0:4], osq[:, 2 * t, :].rearrange("p (h c) -> p h c", c=2 * HD), AX.X, ALU.add)
                    V.tensor_reduce(oss[:, t, 4:12], osq[:, 2 * t + 1, :].rearrange("p (h c) -> p h c", c=HD), AX.X, ALU.add)
                    gap().then_inc(o_ss, 1)
                    dve.wait_ge(o_r, l * TT + t + 1)
                    o_da = xn[:, t, 0:HALF].rearrange("p (h c) -> p h c", c=2 * HD)
                    o_sb = xn[:, t, HALF:].rearrange("p (h c) -> p h c", c=HD)
                    V.tensor_tensor(o_da, ps[DAO_BANK[t]][:, :].rearrange("p (h c) -> p h c", c=2 * HD),
                                    oss[:, t, 12:16].unsqueeze(2).broadcast_to([P, 4, 2 * HD]), ALU.mult)
                    V.tensor_tensor(o_sb, ps[SBO_BANK[t]][:, :].rearrange("p (h c) -> p h c", c=HD),
                                    oss[:, t, 16:24].unsqueeze(2).broadcast_to([P, 8, HD]), ALU.mult)
                    gap()
                    V.scalar_tensor_tensor(o_da, o_da, 1.0 - lam_init, over(dag[:, :], 4), ALU.mult, ALU.mult)
                    V.tensor_tensor(o_sb, o_sb, over(sbg[:, :], 8), ALU.mult)
                    gap().then_inc(o_ready, 1)
                    oT_half(l, t)
                for t in range(TT):
                    for h in range(2):
                        dve.wait_ge(oproj_ps, l * 4 + 2 * t + h + 1)
                        if t == TT - 1:
                            dve.sem_inc(slot_used, 1)
                        c = slice(h * HALF, (h + 1) * HALF)
                        V.tensor_tensor(x_sb[:, t, c], x_sb[:, t, c], ps[OP_BANK[t][h]][:, :], ALU.add).then_inc(x_attn, 1)
                        if t == 1 and h == 0:
                            hT_half(2 * l + 1, 0, g2T)
                            normed(l, 0)
                hT_half(2 * l + 1, 1, g2T)
                normed(l, 1)
                dve.wait_ge(lg_ps, l + 1)
                for t in range(TT):
                    V.scalar_tensor_tensor(lg[:, t, :], ps[4][:, t * 64:t * 64 + GROUPS + EXPERTS], rstd[:, t:t + 1],
                                           br[:, :], ALU.mult, ALU.add)
                gap()
                gl = lg[:, :, 0:GROUPS]
                el = em[:, :, :].rearrange("p t (g e) -> p (t g) e", g=GROUPS)
                first_e, second_e, rest_e = [b[:, :, :].rearrange("p t (g e) -> p (t g) e", g=GROUPS) for b in (oh1, oh2, ev)]
                group = r4[:, 2]
                group_flat = group.rearrange("p t g -> p (t g)")
                rev = cst[:, C_REV:C_OFF]

                def each(ap, n):
                    return ap.unsqueeze(2).broadcast_to([P, ap.shape[1], n])
                V.tensor_copy(em[:, :, :], lg[:, :, GROUPS:])
                V.tensor_reduce(rs[:, 0, :], gl, AX.X, ALU.max)
                gap()
                V.tensor_reduce(rg4[:, 0, :], el, AX.X, ALU.max)
                V.tensor_tensor(r4[:, 0], gl, each(rs[:, 0, :], GROUPS), ALU.subtract).then_inc(rt_diff, 1)
                V.tensor_tensor(group, gl, each(rs[:, 0, :], GROUPS), ALU.is_equal)
                gap()
                V.tensor_tensor(first_e, el, each(rg4[:, 0, :], PER_GROUP), ALU.is_equal)
                V.tensor_tensor(group, group, over(rev[:, 0:GROUPS], TT), ALU.mult)
                gap()
                V.tensor_tensor(first_e, first_e, over(rev[:, 0:PER_GROUP], TT * GROUPS), ALU.mult)
                V.tensor_reduce(rs[:, 7, :], group, AX.X, ALU.max)
                gap()
                V.tensor_reduce(rg4[:, 1, :], first_e, AX.X, ALU.max)
                V.tensor_tensor(group, group, each(rs[:, 7, :], GROUPS), ALU.is_equal)
                gap()
                V.tensor_tensor(first_e, first_e, each(rg4[:, 1, :], PER_GROUP), ALU.is_equal)
                gap()
                V.scalar_tensor_tensor(rest_e, first_e, 3 * NEG, el, ALU.mult, ALU.add)
                gap()
                V.tensor_reduce(rg4[:, 2, :], rest_e, AX.X, ALU.max)
                gap()
                V.tensor_tensor(second_e, rest_e, each(rg4[:, 2, :], PER_GROUP), ALU.is_equal)
                V.tensor_tensor(rg4[:, 3, :], rg4[:, 2, :], rg4[:, 0, :], ALU.subtract)
                gap()
                V.tensor_tensor(second_e, second_e, over(rev[:, 0:PER_GROUP], TT * GROUPS), ALU.mult)
                V.tensor_tensor(r4[:, 3], rg4[:, 3, :].rearrange("p (t g) -> p t g", t=TT), group, ALU.mult)
                V.tensor_tensor(first_e, first_e, each(group_flat, PER_GROUP), ALU.mult)
                gap()
                V.tensor_reduce(rg4[:, 1, :], second_e, AX.X, ALU.max)
                V.tensor_reduce(rs[:, 4, :], r4[:, 3], AX.X, ALU.add).then_inc(rt_diff, 1)
                gap()
                V.tensor_tensor(second_e, second_e, each(rg4[:, 1, :], PER_GROUP), ALU.is_equal)
                gap()
                V.tensor_tensor(second_e, second_e, each(group_flat, PER_GROUP), ALU.mult)
                gap()
                V.tensor_tensor(asg[:, 0:TT, :], oh1[:, :, :], oh2[:, :, :], ALU.add)
                gap().then_inc(rt_asg, 1)
                V.tensor_tensor(asg[:, TT, :], asg[:, 0, :], asg[:, 1, :], ALU.add).then_inc(rt_asg, 1)
                dve.wait_ge(rt_exp, 2 * l + 2)
                V.tensor_reduce(rs[:, 3, :], r4[:, 1], AX.X, ALU.add)
                V.tensor_scalar(rs[:, 6, :], rs[:, 5, :], 1.0, None, ALU.add)
                gap()
                V.tensor_tensor(rs[:, 3, :], rs[:, 3, :], rs[:, 6, :], ALU.mult)
                dve.wait_ge(pos_ps, l + 1)
                V.scalar_tensor_tensor(pos[:, :, 0:EXPERTS], ps[5][:, 0:2 * EXPERTS].rearrange("p (t e) -> p t e", t=TT), 1.0,
                                       asg[:, 0:TT, :], ALU.add, ALU.mult)
                gap()
                select_slots(first, [pos[:, t, 0:LANES] for t in range(TT)], sel)
                V.tensor_reduce(cntf[:, :], ps[5][:, 2 * EXPERTS:3 * EXPERTS].rearrange("p (g j) -> p g j", j=LANES),
                                AX.X, ALU.max)
                V.reciprocal(rs[:, 3, :], rs[:, 3, :])
                gap()
                V.tensor_copy(cnt[:, :], cntf[:, :])
                V.tensor_tensor(rs[:, 6, :], rs[:, 3, :], rs[:, 5, :], ALU.mult)
                gap()
                for t in range(TT):
                    V.tensor_scalar(wgt[:, t, 0:EXPERTS], oh1[:, t, :], rs[:, 3, t:t + 1], None, ALU.mult)
                gap()
                for t in range(TT):
                    V.scalar_tensor_tensor(wgt[:, t, 0:EXPERTS], oh2[:, t, :], rs[:, 6, t:t + 1], wgt[:, t, 0:EXPERTS],
                                           ALU.mult, ALU.add)
                gap().then_inc(routed, 1)
                select_weights(first, [wgt[:, t, 0:LANES] for t in range(TT)], sel, selw)
                gather_copy(first, l * GATHERS + 1, hgT, selwT2[0], 6)
                with dve.Fori(0, SETS // 2) as pair:
                    for parity in range(2):
                        expert_set(l, dve.snap(pair * 2 + parity), parity)
                gap().then_inc(x_done, 1)

        @block.tensor
        def _(pe):
            MM, TR = nc.tensor.matmul, nc.tensor.transpose

            def transpose_x(t):
                for k in range(KC):
                    last = TR(ps[2 * t + k // 4][:, (k % 4) * P:(k % 4 + 1) * P], x_chunked[:, t, k, :], ident)
                    if k % 4 == 3:
                        last.then_inc(hT_ps, 1)

            def block_of(l, i):
                return wbuf[:, block_slot(l, i) * SLOT:(block_slot(l, i) + 1) * SLOT].rearrange("p (k c) -> p k c", k=KC)

            def proj_tile(l, i, t):
                if t == 0:
                    pe.wait_ge(block_in[i], (l + 1) * 16)
                if i == 0:
                    pe.wait_ge(hT_d, 2 * l * TT + t + 1)
                    pe.wait_ge(hT_a, 2 * l * TT + t + 1)
                if i >= 2:
                    before = i - 1 if i == 5 else i - 2
                    pe.wait_ge(proj_out, l * 12 + tile_number(before, t))
                w = block_of(l, i)
                for k in range(KC):
                    if i == 0 and k == KC // 2:
                        pe.wait_ge(block0_rest_in, (l + 1) * 16)
                    last = MM(ps[PROJ_BANK[i][t]][:, :], hT[:, k, t * P:(t + 1) * P], w[:, k, :],
                              start=(k == 0), stop=(k == KC - 1))
                last.then_inc(proj_ps, 1)

            def proj(l, i):
                for t in range(TT):
                    proj_tile(l, i, t)

            def transpose_qk(l, i):
                if i < 2:
                    pe.wait_ge(qk_normed, l * 2 + i + 1)
                else:
                    pe.wait_ge(proj_out, l * 12 + 2 * i + 2)
                if i == 0:
                    pe.wait_ge(hT_a, 2 * l * TT + TT)
                    pe.wait_ge(hT_d, 2 * l * TT + TT)
                if i >= 2:
                    pe.wait_ge(da_max, l * 3 + i)
                for t in range(TT):
                    for a in range(PAIRS):
                        last = TR(ps[QKT_BANK[i][t]][:, a * P:(a + 1) * P], stage[:, i % 2, t, a * P:(a + 1) * P], ident)
                    last.then_inc(qkT_ps, 1)

            def da_scores(l, u):
                keys = P if u == 0 else 2 * P
                heads = HALF // keys
                q0 = 0 if u == 0 else P
                a0 = 2 if u == 2 else 0
                for h in range(heads):
                    for e in range(2):
                        rows = slice(e * HD, (e + 1) * HD)
                        mm = MM(ps[DAS_BANK[u][e]][:, h * keys:(h + 1) * keys], qk[rows, 0, a0 + h, q0:q0 + P],
                                qk[rows, 1, a0 + h, 0:keys], start=True, stop=True)
                        if h == heads - 1:
                            mm.then_inc(da_ps, 1)

            def sb_scores(l, we, wo):
                kt = 1 if we >= 4 else 0
                heads = 4 if kt else 2
                a0 = we if not kt else 0
                for h in range(heads):
                    for e, w in enumerate((we, wo)):
                        rows = slice(e * HD, (e + 1) * HD)
                        n = SEQ - kt * P
                        mm = MM(ps[SB_BANK[w]][:, h * n:(h + 1) * n], qk[rows, 3, a0 + h, kt * P:(kt + 1) * P],
                                qk[rows, 2, a0 + h, kt * P:SEQ], start=True, stop=True)
                        if h == heads - 1:
                            mm.then_inc(sb_ps, 1)

            def da_transpose(l, u):
                pe.wait_ge(da_mix, l * 3 + u + 1)
                for b in range(4):
                    last = TR(ps[DAT_BANK[u]][:, b * P:(b + 1) * P], s_da[:, u, 0, b * P:(b + 1) * P], ident)
                last.then_inc(daT_ps, 1)

            def cumulate(l, w):
                pe.wait_ge(sb_sp, l * 6 + SB_ORDER.index(w) + 1)
                last = MM(ps[SB_BANK[w]][:, :], tri_ge, sp[w], start=True, stop=(w >= 4))
                if w < 4:
                    last = MM(ps[SB_BANK[w]][:, :].rearrange("p (h q) -> p h q", h=2)[:, :, P:], ones,
                       sp[4 + w % 2][:, (w // 2) * 2 * P:(w // 2 + 1) * 2 * P].rearrange("p (h q) -> p h q", h=2),
                       start=False, stop=True)
                last.then_inc(sb_cum, 1)

            def attend(l, t):
                pe.wait_ge(sb_arg, l * 6 + 2)
                pe.wait_ge(proj_out, l * 12 + tile_number(5, t))
                for a in range(PAIRS):
                    for kt in range(t + 1):
                        p = aT[0][:, a, :] if t == 0 else aT[1 + a // 2][:, 2 * (a % 2) + kt, :]
                        MM(ps[DAO_BANK[t]][:, a * P:(a + 1) * P], p, v_sb[:, kt, 0, a * P:(a + 1) * P],
                           start=(kt == 0), stop=(kt == t))
                pe.wait_ge(sb_a, l * 6 + 6)
                for hh in range(2 * PAIRS):
                    a, e = hh // 2, hh % 2
                    cols = slice(hh * HD, (hh + 1) * HD)
                    early = zm[:, 2 * (a // 2) + e, (a % 2) * SEQ:(a % 2 + 1) * SEQ]
                    last = MM(ps[SBO_BANK[t]][:, cols], early[:, t * P:(t + 1) * P], v_sb[:, 0, 1, cols],
                       start=True, stop=(t == 0))
                    if t == 1:
                        last = MM(ps[SBO_BANK[t]][:, cols], zm[:, 4 + e, a * P:(a + 1) * P], v_sb[:, 1, 1, cols],
                           start=False, stop=True)
                last.then_inc(o_ps, 1)

            def transpose_o(l, t):
                pe.wait_ge(o_ready, l * TT + t + 1)
                for k in range(KC):
                    last = TR(ps[OT_BANK[t][k // 4]][:, (k % 4) * P:(k % 4 + 1) * P], xn[:, t, k * P:(k + 1) * P], ident)
                    if k % 4 == 3:
                        last.then_inc(oT_ps, 1)

            def out_proj(l, t, h):
                pe.wait_ge(oT_d, l * TT + t + 1)
                pe.wait_ge(oT_a, l * TT + t + 1)
                i = len(ORDER) + h
                pe.wait_ge(block_in[i], (l + 1) * 16)
                w = block_of(l, i)
                for k in range(KC):
                    last = MM(ps[OP_BANK[t][h]][:, :], hT[:, k, t * P:(t + 1) * P], w[:, k, :],
                              start=(k == 0), stop=(k == KC - 1))
                last.then_inc(oproj_ps, 1)

            def router(l, t):
                pe.wait_ge(hT_d, (2 * l + 1) * TT + t + 1)
                pe.wait_ge(hT_a, (2 * l + 1) * TT + t + 1)
                for k in range(KC):
                    last = MM(ps[4][:, t * 64:t * 64 + GROUPS + EXPERTS], hT[:, k, t * P:(t + 1) * P], wr[:, k, :],
                              start=(k == 0), stop=(k == KC - 1))
                if t == TT - 1:
                    last.then_inc(lg_ps, 1)

            def keep_clock(n, operand=ident):
                for _ in range(n):
                    MM(ps[7][:, 0:P], operand, operand, start=True, stop=True)

            def ranks(l):
                pe.wait_ge(rt_asg, 2 * l + 1)
                MM(ps[5][:, 0:TT * EXPERTS], tri_lt, asg[:, 0:TT, :], start=True, stop=False)
                MM(ps[5][:, EXPERTS:2 * EXPERTS], ones, asg[:, 0, :], start=False, stop=True)
                pe.wait_ge(rt_asg, 2 * l + 2)
                MM(ps[5][:, 2 * EXPERTS:3 * EXPERTS], ones, asg[:, TT, :], start=True, stop=True).then_inc(pos_ps, 1)

            def gather(s, n, sel=sel):
                pe.wait_ge(s["sel_ready"], n)
                for k in range(KC):
                    for t in range(TT):
                        last = MM(ps[k // 4][:, (k % 4) * P:(k % 4 + 1) * P], xn[:, t, k * P:(k + 1) * P], sel[:, t, :],
                                  start=(t == 0), stop=(t == TT - 1))
                last.then_inc(s["gathered"], 1)

            def transpose_weights(s, n, bank, selw=selw):
                pe.wait_ge(s["selw_ready"], n)
                for t in range(TT):
                    last = TR(ps[bank][:, t * P:(t + 1) * P], selw[:, t, :], ident)
                last.then_inc(s["selwT_ps"], 1)

            halves = wbuf[:, :].rearrange("p (n k f) -> p n k f", k=KC, f=FF)

            def gate_up(s, n, src, l, parity):
                pe.wait_ge(s["hg_d"], n)
                pe.wait_ge(s["hg_a"], n)
                for k in range(KC):
                    for j in range(LANES):
                        gate, up = 2 * lane_slot(l, parity, j), up_at(l, parity, j) * 2 // SLOT
                        MM(ps[2][j * SLOTS:(j + 1) * SLOTS, :].rearrange("p (a f) -> p a f", a=2),
                           src[:, k, j * SLOTS:(j + 1) * SLOTS], halves[:, gate:up + 1:up - gate, k, :],
                           start=(k == 0), stop=(k == KC - 1))
                pe.drain().then_inc(s["gu_ps"], 1)

            def transpose_act(s, n):
                pe.wait_ge(s["act_out"], n)
                for c in range(FC):
                    last = TR(ps[3][:, c * P:(c + 1) * P], act_sb[:, c * P:(c + 1) * P], ident)
                last.then_inc(s["actT_ps"], 1)

            def down(s, l, last):
                at = [wbuf[:, last_down_at(l, j):last_down_at(l, j) + SLOT // 2] if last else dnbuf[:, j, :]
                      for j in range(LANES)]
                for h in range(2):
                    for c in range(FC):
                        for j in range(LANES):
                            MM(ps[4 + h][j * SLOTS:(j + 1) * SLOTS, :], actT[:, c, j * SLOTS:(j + 1) * SLOTS],
                               at[j][:, c * D + h * HALF:c * D + (h + 1) * HALF], start=(c == 0), stop=(c == FC - 1))
                    pe.drain().then_inc(s[f"dn{h}_ps"], 1)

            def scatter(s, n, weights):
                pe.wait_ge(s["y_d"], n)
                pe.wait_ge(s["y_a"], n)
                for t in range(TT):
                    for h in range(2):
                        last = MM(ps[SC_BANK[t][h]][:, :], weights[:, t, :], y[:, h * HALF:(h + 1) * HALF], start=True, stop=True)
                    last.then_inc(s[f"sc{t}_ps"], 1)

            def expert_set(l, g, parity, last):
                for j in range(LANES):
                    pe.wait_ge(gu_in[parity][j], g * 16 + (l * SETS + 2 - parity) * 16)
                gate_up(first, g + (l * GATHERS + 1), hgT, l, parity)
                most = pe.value_load(cnt[0:1, bass.ds(g, 1)], min_val=0, max_val=SEQ)
                n = pe.snap(g + l * SETS + 1)
                with pe.If(most <= SLOTS):
                    pe.sem_inc(slot_used, LANES)
                following = pe.snap(g + l * GATHERS + 2)
                gather(first, following)
                pe.wait_ge(x_moe, g + (l * SETS + 1))
                pe.wait_ge(x_more, g * MORE + (l * SETS * MORE + 1))
                pe.wait_ge(first["selwT_out"], g + (l * GATHERS + 1))
                transpose_weights(first, following, 6)
                transpose_act(first, n)

                def early(m):
                    pe.wait_ge(first["hg_d"], g + (l * GATHERS + 2))
                    pe.wait_ge(first["hg_a"], g + (l * GATHERS + 2))
                    gather(more, m, sel_more)
                    transpose_weights(more, m, 7, selw_more)
                    gate_up(more, m, hgT_more, l, parity)
                    pe.wait_ge(more["selwT_out"], m)
                    with pe.If(most <= 2 * SLOTS):
                        pe.sem_inc(slot_used, LANES)

                def late(m):
                    pe.wait_ge(more["actT_out"], m)
                    pe.wait_ge(x_moe0, n)
                    down(more, l, last)
                    with pe.If(most <= 2 * SLOTS):
                        pe.sem_inc(dn_used, 1)
                    pe.wait_ge(x_moe, g + (l * SETS + 2))
                    scatter(more, m, selwT_more)

                def whole(m, r):
                    pe.wait_ge(x_more, m)
                    gather(more, m, sel_more)
                    transpose_weights(more, m, 7, selw_more)
                    gate_up(more, m, hgT_more, l, parity)
                    transpose_act(more, m)
                    pe.wait_ge(more["actT_out"], m)
                    down(more, l, last)
                    pe.wait_ge(more["selwT_out"], m)
                    scatter(more, m, selwT_more)

                second_round_early(pe, g + l * SETS, most, early)
                for j in range(LANES):
                    if last:
                        pe.wait_ge(dn_last_in[j], (l + 1) * 16)
                    else:
                        pe.wait_ge(dn_in[j], g * 16 + (l * (SETS - 1) + 1) * 16)
                pe.wait_ge(first["actT_out"], n)
                down(first, l, last)
                with pe.If(most <= SLOTS):
                    pe.sem_inc(dn_used, 1)
                with pe.If(most > SLOTS):
                    transpose_act(more, pe.snap(g * MORE + (l * SETS * MORE + 1)))
                pe.wait_ge(first["selwT_out"], g + (l * GATHERS + 2))
                scatter(first, n, selwT2[parity])
                further_rounds(pe, g + l * SETS, most, late, whole, PE_MORE)
                with pe.If(most > 2 * SLOTS):
                    pe.sem_inc(slot_used, LANES)
                    pe.sem_inc(dn_used, 1)

            x_chunked = x_sb[:, :, :].rearrange("p t (c k) -> p t k c", k=KC)
            pe.wait_ge(zeros_ready, 1)
            keep_clock(8, xn[:, 0, 0:P])
            pe.wait_ge(ident_in, 16)
            for l in range(DEPTH):
                if l > 0:
                    pe.wait_ge(x_done, l)
                for t in range(TT):
                    if l == 0:
                        pe.wait_ge(x_in[t], 16)
                    transpose_x(t)
                proj(l, 0)
                proj(l, 1)
                transpose_qk(l, 0)
                proj(l, 2)
                transpose_qk(l, 1)
                proj_tile(l, 3, 0)
                pe.wait_ge(qkT_d, l * 4 + 2)
                pe.wait_ge(qkT_a, l * 4 + 2)
                da_scores(l, 0)
                da_scores(l, 1)
                proj_tile(l, 3, 1)
                pe.wait_ge(da_max, l * 3 + 1)
                da_scores(l, 2)
                transpose_qk(l, 2)
                pe.wait_ge(proj_out, l * 12 + 8)
                da_transpose(l, 0)
                da_transpose(l, 1)
                transpose_qk(l, 3)
                pe.wait_ge(qkT_d, l * 4 + 4)
                pe.wait_ge(qkT_a, l * 4 + 4)
                sb_scores(l, 4, 5)
                sb_scores(l, 0, 1)
                proj_tile(l, 4, 0)
                pe.wait_ge(daT_out, l * 3 + 1)
                da_transpose(l, 2)
                if l == 0:
                    pe.wait_ge(const_in, 16)
                cumulate(l, 4)
                cumulate(l, 5)
                pe.wait_ge(daT_out, l * 3 + 3)
                sb_scores(l, 2, 3)
                proj_tile(l, 5, 0)
                for w in range(4):
                    cumulate(l, w)
                proj_tile(l, 4, 1)
                attend(l, 0)
                proj_tile(l, 5, 1)
                transpose_o(l, 0)
                attend(l, 1)
                out_proj(l, 0, 0)
                transpose_o(l, 1)
                out_proj(l, 0, 1)
                out_proj(l, 1, 0)
                pe.wait_ge(x_attn, l * 2 * TT + 2)
                transpose_x(0)
                out_proj(l, 1, 1)
                pe.wait_ge(x_attn, l * 2 * TT + 4)
                transpose_x(1)
                router(l, 0)
                router(l, 1)
                keep_clock(12)
                ranks(l)
                keep_clock(4)
                gather(first, l * GATHERS + 1)
                transpose_weights(first, l * GATHERS + 1, 6)
                pe.wait_ge(routed, l + 1)
                with pe.Fori(0, SETS // 2 - 1) as pair:
                    expert_set(l, pe.snap(pair * 2), 0, False)
                    expert_set(l, pe.snap(pair * 2 + 1), 1, False)
                with pe.Fori(SETS // 2 - 1, SETS // 2) as pair:
                    expert_set(l, pe.snap(pair * 2), 0, False)
                    expert_set(l, pe.snap(pair * 2 + 1), 1, True)


NAMES = ["x", "norm1_g", "w_in", "q_norm_g", "k_norm_g", "lambda_q1", "lambda_k1", "lambda_q2", "lambda_k2",
         "da_out_g", "sb_out_g", "w_out", "norm2_g", "w_router_group", "b_router_group", "w_router_expert",
         "b_router_expert", "w_gate", "w_up", "w_down"]


def kernel(**inputs):
    import concourse.bacc as bacc
    from concourse.bass_utils import run_bass_kernel_spmd

    nc = bacc.Bacc("TRN2", target_bir_lowering=False, num_devices=1)
    arrays = {"in_const": shape_constants()}
    arrays |= {f"in_{n}": np.ascontiguousarray(inputs[n]) for n in NAMES}
    aps = [nc.dram_tensor(n, a.shape, mybir.dt.from_np(a.dtype), kind="ExternalInput").ap() for n, a in arrays.items()]
    out = nc.dram_tensor("out_0", (1, SEQ, D), F32, kind="ExternalOutput").ap()
    decoder(nc, *aps, out)
    return run_bass_kernel_spmd(nc, [arrays], core_ids=[0]).results[0]["out_0"]
```
